# Optimizing a Trainium2 kernel written in Bass

```python
import math
import jax, jax.numpy as jnp
from jax import lax
import numpy as np

D_MODEL = 1024
BATCH = 1
SEQ = 256
DEPTH = 2
DEC_BATCH = 1
DEC_SEQ = 256
PAST_LEN = 128

GRID_W = 64
D_FF = 2816
N_EVEN = (DEPTH + 1) // 2
N_ODD = DEPTH // 2
EPS = 1e-6
POOL_WIDTH = D_MODEL // 2
POOL_GROUPS = 4
POOL_GROUP_W = POOL_WIDTH // POOL_GROUPS
POOL_WINDOWS = (2, 4, 8, 16)
HYENA_WIDTH = D_MODEL // 2
HYENA_BANDS = 16
HYENA_EMB = 1 + 2 * HYENA_BANDS
HYENA_FILTER_HIDDEN = 64
HYENA_SHORT = 3
HYENA_MOD_SHIFT = 0.05
HYENA_DECAY_TARGET = 1e-2
HYENA_FAST_DECAY_PCT = 0.3
HYENA_SLOW_DECAY_PCT = 1.5
AB_IN = POOL_WIDTH + 3 * HYENA_WIDTH
AB_OUT = POOL_WIDTH + HYENA_WIDTH
N_HEADS = 16
HEAD_DIM = D_MODEL // N_HEADS
NA_MAX_ROWS = 8
NA_COLS = 16

kernel_name = "hybrid_pool_hyena_natten_encoder"

def rmsnorm(x, g):
    xf = x.astype(jnp.float32)
    y = xf * lax.rsqrt(jnp.mean(xf * xf, axis=-1, keepdims=True) + EPS)
    return (y * g.astype(jnp.float32)).astype(x.dtype)

def swiglu(x, wg, wu, wd):
    return (jax.nn.silu(x @ wg) * (x @ wu)) @ wd

def pool_mixer(u, w_grp, scale):
    B, L, _ = u.shape
    t = np.arange(L)[:, None]
    w = np.array(POOL_WINDOWS)[None, :]
    lo = np.clip(t - w // 2, 0, L - 1)
    hi = np.clip(t + w - w // 2 - 1, 0, L - 1)
    cnt = (hi - lo + 1).astype(np.float32)
    gidx = np.arange(POOL_GROUPS)[None, :]
    uf = u.astype(jnp.float32).reshape(B, L, POOL_GROUPS, POOL_GROUP_W)
    cs = jnp.concatenate([jnp.zeros((B, 1, POOL_GROUPS, POOL_GROUP_W), jnp.float32),
                          jnp.cumsum(uf, axis=1)], axis=1)
    win_sum = cs[:, hi + 1, gidx, :] - cs[:, lo, gidx, :]
    pooled = (win_sum / cnt[None, :, :, None] - uf).astype(u.dtype)
    mixed = jnp.einsum('blgc,gcd->blgd', pooled, w_grp)
    return mixed.reshape(B, L, POOL_WIDTH) * scale

def short_conv(u, w, b):
    up = jnp.pad(u, ((0, 0), (1, 1), (0, 0)))
    return up[:, :-2] * w[0] + up[:, 1:-1] * w[1] + up[:, 2:] * w[2] + b

def hyena_filter_fft(L, w1, b1, w2, b2, w3, b3, freq, w_out, deltas):
    t_idx = jnp.arange(L, dtype=jnp.float32)
    t_norm = jnp.linspace(0.0, 1.0, L, dtype=jnp.float32)
    bands = jnp.linspace(1e-4, HYENA_BANDS - 1, HYENA_BANDS, dtype=jnp.float32)
    ang = (2.0 * math.pi / L) * t_idx[:, None] * bands[None, :]
    z = jnp.concatenate([t_norm[:, None], jnp.cos(ang), -jnp.sin(ang)], axis=-1)
    h = jnp.sin(freq * (z @ w1 + b1))
    h = jnp.sin(freq * (h @ w2 + b2))
    h = jnp.sin(freq * (h @ w3 + b3))
    h = (h @ w_out).astype(jnp.float32)
    decay = jnp.exp(-t_norm[:, None] * jnp.abs(deltas.astype(jnp.float32)))
    h = (h * (decay + HYENA_MOD_SHIFT)).reshape(L, 2, HYENA_WIDTH)
    k = jnp.concatenate([h[:, 0], jnp.zeros((1, HYENA_WIDTH), jnp.float32), h[:0:-1, 1]], axis=0)
    return jnp.fft.rfft(k, axis=0)

def fftconv(u, k_f, bias):
    L = u.shape[1]
    uf = u.astype(jnp.float32)
    y = jnp.fft.irfft(jnp.fft.rfft(uf, n=2 * L, axis=1) * k_f[None], n=2 * L, axis=1)[:, :L]
    return y + uf * bias.astype(jnp.float32)

def pool_hyena_mixer(xn, w_in, pool_w, pool_scale, short_w, short_b, fw1, fb1, fw2, fb2, fw3, fb3,
                     ffreq, fw_out, fdeltas, h_bias, w_out):
    L = xn.shape[1]
    p = xn @ w_in
    a = pool_mixer(p[..., :POOL_WIDTH], pool_w, pool_scale)
    hb = short_conv(p[..., POOL_WIDTH:], short_w, short_b)
    x0 = hb[..., :HYENA_WIDTH]
    x1 = hb[..., HYENA_WIDTH:2 * HYENA_WIDTH]
    v = hb[..., 2 * HYENA_WIDTH:]
    k_f = hyena_filter_fft(L, fw1, fb1, fw2, fb2, fw3, fb3, ffreq, fw_out, fdeltas)
    yh = (fftconv(v * x1, k_f, h_bias) * x0.astype(jnp.float32)).astype(xn.dtype)
    return jnp.concatenate([a, yh], axis=-1) @ w_out

def na_mixer(xn, w_qkv, gq, gk, rpb, w_o):
    B, L, _ = xn.shape
    rows = L // GRID_W
    kh = min(NA_MAX_ROWS, rows)
    qkv = (xn @ w_qkv).reshape(B, L, 3, N_HEADS, HEAD_DIM)
    q = rmsnorm(qkv[:, :, 0], gq)
    k = rmsnorm(qkv[:, :, 1], gk)
    v = qkv[:, :, 2]

    def to_grid(a):
        return a.reshape(B, rows, GRID_W, N_HEADS, HEAD_DIM).transpose(0, 3, 1, 2, 4)

    qg, kg, vg = to_grid(q), to_grid(k), to_grid(v)
    c = np.arange(GRID_W)
    c_start = np.clip(c - NA_COLS // 2, 0, GRID_W - NA_COLS)
    col_mask = (c[None, :] >= c_start[:, None]) & (c[None, :] < c_start[:, None] + NA_COLS)
    dc_idx = np.clip(c[None, :] - c[:, None] + NA_COLS - 1, 0, 2 * NA_COLS - 2)
    rpb_cols = rpb[:, :, dc_idx].astype(jnp.float32)
    scale = HEAD_DIM ** -0.5

    def one_row(r):
        s = jnp.clip(r - kh // 2, 0, rows - kh)
        k_blk = lax.dynamic_slice_in_dim(kg, s, kh, axis=2)
        v_blk = lax.dynamic_slice_in_dim(vg, s, kh, axis=2)
        q_r = lax.dynamic_index_in_dim(qg, r, axis=2, keepdims=False)
        sc = jnp.einsum('bhqd,bhikd->bhqik', q_r, k_blk, preferred_element_type=jnp.float32) * scale
        dr = s + jnp.arange(kh) - r + NA_MAX_ROWS - 1
        bias = jnp.take(rpb_cols, dr, axis=1).transpose(0, 2, 1, 3)
        sc = jnp.where(col_mask[:, None, :], sc + bias, -jnp.inf)
        p = jax.nn.softmax(sc, axis=(-2, -1))
        return jnp.einsum('bhqik,bhikd->bhqd', p.astype(v_blk.dtype), v_blk)

    out = lax.map(one_row, jnp.arange(rows))
    out = out.transpose(1, 0, 3, 2, 4).reshape(B, L, D_MODEL)
    return out @ w_o

def run_trunk(x, norm_g, ffn_w_gate, ffn_w_up, ffn_w_down, w_in_ab, pool_w, pool_scale, short_w, short_b,
              filt_w1, filt_b1, filt_w2, filt_b2, filt_w3, filt_b3, filt_freq, filt_w_out, filt_deltas,
              hyena_bias, w_out_ab, w_qkv, q_norm_g, k_norm_g, rpb, w_o):
    for layer in range(DEPTH):
        x = x + 0.5 * swiglu(rmsnorm(x, norm_g[layer, 0]), ffn_w_gate[layer, 0], ffn_w_up[layer, 0], ffn_w_down[layer, 0])
        xn = rmsnorm(x, norm_g[layer, 1])
        i = layer // 2
        if layer % 2 == 0:
            mix = pool_hyena_mixer(xn, w_in_ab[i], pool_w[i], pool_scale[i], short_w[i], short_b[i],
                                   filt_w1[i], filt_b1[i], filt_w2[i], filt_b2[i], filt_w3[i], filt_b3[i],
                                   filt_freq[i], filt_w_out[i], filt_deltas[i], hyena_bias[i], w_out_ab[i])
        else:
            mix = na_mixer(xn, w_qkv[i], q_norm_g[i], k_norm_g[i], rpb[i], w_o[i])
        x = x + mix
        x = x + 0.5 * swiglu(rmsnorm(x, norm_g[layer, 2]), ffn_w_gate[layer, 1], ffn_w_up[layer, 1], ffn_w_down[layer, 1])
    return x

def setup_inputs(seed: int = 0) -> dict:
    key = jax.random.key(seed)
    ks = jax.random.split(key, 32)

    def nrm(k, shape, s):
        return jax.random.normal(k, shape, jnp.float32) * s

    max_decay = math.log(HYENA_DECAY_TARGET) / HYENA_FAST_DECAY_PCT
    min_decay = math.log(HYENA_DECAY_TARGET) / HYENA_SLOW_DECAY_PCT
    base_deltas = jnp.tile(jnp.linspace(min_decay, max_decay, HYENA_WIDTH, dtype=jnp.float32), 2)
    return {
        "x_prompt": nrm(ks[0], (BATCH, SEQ, D_MODEL), 1.0),
        "x_sample": nrm(ks[1], (DEC_BATCH, DEC_SEQ, D_MODEL), 1.0),
        "norm_g": 1.0 + nrm(ks[2], (DEPTH, 3, D_MODEL), 0.02),
        "ffn_w_gate": nrm(ks[3], (DEPTH, 2, D_MODEL, D_FF), D_MODEL ** -0.5),
        "ffn_w_up": nrm(ks[4], (DEPTH, 2, D_MODEL, D_FF), D_MODEL ** -0.5),
        "ffn_w_down": nrm(ks[5], (DEPTH, 2, D_FF, D_MODEL), D_FF ** -0.5),
        "w_in_ab": nrm(ks[6], (N_EVEN, D_MODEL, AB_IN), D_MODEL ** -0.5),
        "pool_w": nrm(ks[7], (N_EVEN, POOL_GROUPS, POOL_GROUP_W, POOL_GROUP_W), POOL_GROUP_W ** -0.5),
        "pool_scale": 1.0 + nrm(ks[8], (N_EVEN, POOL_WIDTH), 0.02),
        "short_w": nrm(ks[9], (N_EVEN, HYENA_SHORT, 3 * HYENA_WIDTH), HYENA_SHORT ** -0.5),
        "short_b": nrm(ks[10], (N_EVEN, 3 * HYENA_WIDTH), 0.01),
        "filt_w1": nrm(ks[11], (N_EVEN, HYENA_EMB, HYENA_FILTER_HIDDEN), HYENA_EMB ** -0.5),
        "filt_b1": nrm(ks[12], (N_EVEN, HYENA_FILTER_HIDDEN), 0.1),
        "filt_w2": nrm(ks[13], (N_EVEN, HYENA_FILTER_HIDDEN, HYENA_FILTER_HIDDEN), HYENA_FILTER_HIDDEN ** -0.5),
        "filt_b2": nrm(ks[14], (N_EVEN, HYENA_FILTER_HIDDEN), 0.1),
        "filt_w3": nrm(ks[15], (N_EVEN, HYENA_FILTER_HIDDEN, HYENA_FILTER_HIDDEN), HYENA_FILTER_HIDDEN ** -0.5),
        "filt_b3": nrm(ks[16], (N_EVEN, HYENA_FILTER_HIDDEN), 0.1),
        "filt_freq": 1.0 + nrm(ks[17], (N_EVEN, HYENA_FILTER_HIDDEN), 0.1),
        "filt_w_out": nrm(ks[18], (N_EVEN, HYENA_FILTER_HIDDEN, 2 * HYENA_WIDTH), 0.05 * HYENA_FILTER_HIDDEN ** -0.5),
        "filt_deltas": base_deltas[None, :] + nrm(ks[19], (N_EVEN, 2 * HYENA_WIDTH), 0.1),
        "hyena_bias": nrm(ks[20], (N_EVEN, HYENA_WIDTH), 0.1),
        "w_out_ab": nrm(ks[21], (N_EVEN, AB_OUT, D_MODEL), AB_OUT ** -0.5),
        "w_qkv": nrm(ks[22], (N_ODD, D_MODEL, 3 * D_MODEL), D_MODEL ** -0.5),
        "q_norm_g": 1.0 + nrm(ks[23], (N_ODD, HEAD_DIM), 0.02),
        "k_norm_g": 1.0 + nrm(ks[24], (N_ODD, HEAD_DIM), 0.02),
        "rpb": nrm(ks[25], (N_ODD, N_HEADS, 2 * NA_MAX_ROWS - 1, 2 * NA_COLS - 1), 0.1),
        "w_o": nrm(ks[26], (N_ODD, D_MODEL, D_MODEL), D_MODEL ** -0.5),
    }

def reference(x_prompt, x_sample, norm_g, ffn_w_gate, ffn_w_up, ffn_w_down, w_in_ab, pool_w, pool_scale,
              short_w, short_b, filt_w1, filt_b1, filt_w2, filt_b2, filt_w3, filt_b3, filt_freq, filt_w_out,
              filt_deltas, hyena_bias, w_out_ab, w_qkv, q_norm_g, k_norm_g, rpb, w_o):
    y_prompt = run_trunk(x_prompt, norm_g, ffn_w_gate, ffn_w_up, ffn_w_down, w_in_ab, pool_w, pool_scale,
                         short_w, short_b, filt_w1, filt_b1, filt_w2, filt_b2, filt_w3, filt_b3, filt_freq,
                         filt_w_out, filt_deltas, hyena_bias, w_out_ab, w_qkv, q_norm_g, k_norm_g, rpb, w_o)
    y_sample = run_trunk(x_sample, norm_g, ffn_w_gate, ffn_w_up, ffn_w_down, w_in_ab, pool_w, pool_scale,
                         short_w, short_b, filt_w1, filt_b1, filt_w2, filt_b2, filt_w3, filt_b3, filt_freq,
                         filt_w_out, filt_deltas, hyena_bias, w_out_ab, w_qkv, q_norm_g, k_norm_g, rpb, w_o)
    return (y_prompt, y_sample)


_drawn_inputs = setup_inputs


def setup_inputs(seed=0):
    import zlib

    import numpy as np

    out = dict(_drawn_inputs(seed))
    spreads = {}
    factors = {'norm_g': 2.768,
     'pool_scale': 5.298,
     'short_b': 8.0,
     'filt_b1': 3.796,
     'filt_b2': 3.171,
     'filt_b3': 2.806,
     'filt_freq': 4.735,
     'q_norm_g': 8.0,
     'k_norm_g': 8.0,
     'rpb': 20.663}
    for name, (base, spread) in spreads.items():
        noise = np.random.default_rng([zlib.crc32(name.encode()), seed]).standard_normal(out[name].shape)
        drawn = base * np.exp(spread * noise) if base else spread * noise
        out[name] = __import__('jax').numpy.asarray(drawn.astype(out[name].dtype))
    for name, factor in factors.items():
        out[name] = (out[name] * factor).astype(out[name].dtype)
    return out
```

```python
from contextlib import ExitStack

import numpy as np

import concourse.bass as bass
from concourse import mybir

F32 = mybir.dt.float32
F32R = mybir.dt.float32r
ACT = mybir.ActivationFunctionType
ALU = mybir.AluOpType
AX = mybir.AxisListType

P = 128
D = 1024
KD = D // P
FF = 2816
KF = FF // P
SEQ = 256
NSEQ = 2
TOK = NSEQ * SEQ
TT = TOK // P
EPS = 1e-6
HEADS = 16
HD = 64
PAIRS = HEADS // 2
GRID_W = 64
ROWS = SEQ // GRID_W
RPB_R, RPB_C = 15, 31
DR = 2 * ROWS - 1
NA_COLS = 16
WINDOWS = (2, 4, 8, 16)
HW = 512
KH = HW // P
EMB, HID = 33, 64
NFREQ = SEQ
PAD = 8
PROW = SEQ + 2 * PAD
MAGIC = 1.5 * 2.0 ** 23
TWO_PI = 2.0 * np.pi
PI_A = 6.28125
PI_B = float(np.float32(np.round((TWO_PI - PI_A) * 2.0 ** 21) / 2.0 ** 21))
PI_C = float(np.float32(TWO_PI - PI_A - PI_B))
SIN_MAX = 3.1415925

C_ID, C_HEAD, C_MEAN, C_EPS, C_T, C_MASK, C_ALL = 0, 128, 130, 131, 132, 134, 198
V_NORM, V_PSCALE, V_SW, V_SB, V_GQ, V_GK, V_B1, V_FREQ, V_ALL = 0, 48, 52, 88, 100, 101, 102, 105, 106
UNIT_CREDIT, EVAC_CREDIT, LOW_CREDIT = 2, 2, 3
SCORE_CREDIT, TURN_CREDIT, VALUE_CREDIT, OUT_CREDIT, COPY_CREDIT, STORE_CREDIT = 4, 1, 2, 1, 1, 16


class Phase:

    def __init__(self, name, iters, slots, ktiles, groups_at):
        self.name, self.iters, self.slots, self.kt, self.groups_at = name, iters, slots, ktiles, groups_at
        self.per = slots
        self.gper = len(groups_at)

    def unit(self, i, j):
        return self.unit0 + self.per * i + j

    def group(self, i, j):
        return self.group0 + self.gper * i + self.groups_at.index(j)


def plan():
    up = lambda n: Phase(f"up{n}", KF // 2, 4, KD, [0, 1, 2, 3])
    down = lambda n: Phase(f"down{n}", KD // 2, 4, KF // 2, [1, 3])
    phases = [up(0), down(0), Phase("w_in", KH, 4, KD, [0, 1, 2, 3]), Phase("w_out", 2, 4, KD, [0, 1, 2, 3]),
              up(1), down(1), up(2), down(2), Phase("qkv", PAIRS, 3, KD, [0, 1, 2]),
              Phase("w_o", 2, 4, KD, [0, 1, 2, 3]), up(3), down(3)]
    unit, group, uses = 0, KD, [0] * 4
    for n, ph in enumerate(phases):
        ph.unit0, ph.group0, ph.uses0 = unit, group, list(uses)
        unit += ph.iters * ph.per
        group += ph.iters * ph.gper
        for s in range(ph.slots):
            uses[s] += ph.iters
        ph.next = phases[n + 1] if n + 1 < len(phases) else None
    return phases


def build_trunk(nc, a, y_prompt, y_sample):
    phases = plan()
    by = {ph.name: ph for ph in phases}
    NEXT_NORM = {"down0": 1, "w_out": 2, "down1": 3, "down2": 4, "w_o": 5}
    NEXT_NORM["down1"] = 3
    NORM_OF = {"up0": 0, "w_in": 1, "up1": 2, "up2": 3, "qkv": 4, "up3": 5}
    ffn_of = {"up0": 0, "down0": 0, "up1": 1, "down1": 1, "up2": 2, "down2": 2, "up3": 3, "down3": 3}

    wg = a["ffn_w_gate"].rearrange("l j (k p) f -> (l j) p k f", p=P)
    wu = a["ffn_w_up"].rearrange("l j (k p) f -> (l j) p k f", p=P)
    wd = a["ffn_w_down"].rearrange("l j (k p) d -> (l j) p k d", p=P)
    w_in = a["w_in_ab"].rearrange("o (k p) f -> (o p) k f", p=P)
    w_out = a["w_out_ab"].rearrange("o (k p) f -> (o p) k f", p=P)
    w_qkv = a["w_qkv"].rearrange("o (k p) f -> (o p) k f", p=P)
    w_o = a["w_o"].rearrange("o (k p) f -> (o p) k f", p=P)
    bias_dram = nc.dram_tensor("bias_by_column", [GRID_W, HEADS, DR * GRID_W], F32).ap()

    with ExitStack() as ctx:
        def sb(name, shape, dt=F32, where=ctx):
            return where.enter_context(nc.sbuf_tensor(name, shape, dt))

        def sem(name):
            return ctx.enter_context(nc.semaphore(name))

        x = sb("x", [P, KD, TOK])
        xh = sb("xh", [P, KD, TOK], F32R)
        xl = sb("xl", [P, KD, TOK], F32R)
        raw = [sb(f"raw{s}", [P, KF // 2, P]) for s in range(4)]
        wh = [sb(f"wh{s}", [P, KF // 2, P], F32R) for s in range(2)]
        wl = [sb(f"wl{s}", [P, KF // 2, P], F32R) for s in range(2)]
        rbc = sb("rbc", [P, TOK])
        sqacc = sb("sqacc", [P, TOK])
        sqtmp = sb("sqtmp", [P, 2, TOK])
        ga = [sb(f"ga{s}", [P, TOK]) for s in range(2)]
        ua = [sb(f"ua{s}", [P, TOK]) for s in range(2)]
        rwide = sb("rwide", [P, TT, P])
        rcol = sb("rcol", [P, TT])
        cst = sb("cst", [P, C_ALL])
        vrow = sb("vrow", [V_ALL, P])
        vec = sb("vec", [P, V_ALL])
        gqk = sb("gqk", [P, 1])
        h3 = sb("h3", [HID, SEQ])
        ident = cst[:, C_ID:C_ID + P]

        def region(rows):
            own = ExitStack()
            got = [sb(*r, where=own) for r in rows]
            own.close()
            return got

        hh, hl = region([("hh", [P, KF, TOK], F32R), ("hl", [P, KF, TOK], F32R)])
        xrow, zT, fw1, fw2, fw3, fa, fk, fh = region([
            ("xrow", [P, TT, D]), ("zT", [EMB, SEQ]), ("fw1", [EMB, HID]), ("fw2", [HID, HID]),
            ("fw3", [HID, HID]), ("fa", [HID, SEQ]), ("fk", [HID, SEQ]), ("fh", [HID, SEQ])])
        own = ExitStack()
        dft = sb("dft", [P, 2, 2, NFREQ], where=own)
        idft = sb("idft", [P, 4, SEQ], where=own)
        icnt = sb("icnt", [P, 4, SEQ], where=own)
        kf = sb("kf", [P, 2, 2, HW], where=own)
        x0 = sb("x0", [P, KH, TOK], where=own)
        ppad = sb("ppad", [P, 4, NSEQ, PROW], where=own)
        win = [sb(f"win{s}", [P, NSEQ, PROW], where=own) for s in range(2)]
        up = sb("up", [P, TOK], where=own)
        poolw = sb("poolw", [P, 4, P], where=own)
        inner = ExitStack()
        decay, filt = sb("decay", [P, 2, 2, HW], where=inner), sb("filt", [P, 2, 2, HW], where=inner)
        inner.close()
        spec = sb("spec", [P, NSEQ, 2, 2, HW], where=own)
        inner = ExitStack()
        absd, hsum = sb("absd", [P, 2 * HW], where=inner), sb("hsum", [P, 2, HW], where=inner)
        hdif, ut = sb("hdif", [P, 2, HW], where=inner), sb("ut", [P, TT, HW], where=inner)
        hbias, fwo = sb("hbias", [1, HW], where=inner), sb("fwo", [HID, 2 * HW], where=inner)
        inner.close()
        ah, al = sb("ah", [P, KD, TOK], F32R, where=own), sb("al", [P, KD, TOK], F32R, where=own)
        own.close()
        (wh2, wl2, qt, kt, vt, sqq, sqk, qs, kn, vs, braw, bmask, sc, pt, oh, ol, rsum, nmax, rqk, kwide) = region([
            ("wh2", [P, KD, P], F32R), ("wl2", [P, KD, P], F32R), ("qt", [P, TOK]), ("kt", [P, TOK]), ("vt", [P, TOK]),
            ("sqq", [P, TOK]), ("sqk", [P, TOK]), ("qs", [P, TOK]), ("kn", [P, TOK]), ("vs", [P, TT, P]),
            ("braw", [P, 2, 6 * GRID_W]), ("bmask", [P, 2, 6 * GRID_W]), ("sc", [P, 2, 2, SEQ]), ("pt", [P, 2, 2, SEQ]),
            ("oh", [P, KD, TOK], F32R), ("ol", [P, KD, TOK], F32R), ("rsum", [P, 2, 2]), ("nmax", [P, 2, 2]),
            ("rqk", [P, 2, TT, 2]), ("kwide", [P, TT, P])])
        wh, wl = wh + [wh2], wl + [wl2]

        bank = [ctx.enter_context(nc.psum_tensor(f"bank{b}", [P, TOK], F32)) for b in range(8)]

        raw_in = [sem(f"raw_in{s}") for s in range(4)]
        const_in, vec_in, filt_in, out_in = sem("const_in"), sem("vec_in"), sem("filt_in"), sem("out_in")
        x_in = [sem(f"x_in{s}") for s in range(TT)]
        mix_in, toep_in, braw_in = sem("mix_in"), sem("toep_in"), sem("braw_in")
        high, low, unit_done, evac = sem("high"), sem("low"), sem("unit_done"), sem("evac")
        xh_done, xl_done, sq_done, acc_done = sem("xh_done"), sem("xl_done"), sem("sq_done"), sem("acc_done")
        mean_mm, std_done, rwide_done, rbc_mm, rbc_done = (sem("mean_mm"), sem("std_done"), sem("rwide_done"),
                                                           sem("rbc_mm"), sem("rbc_done"))
        silu_done, h_done, hh_done, hl_done = sem("silu_done"), sem("h_done"), sem("hh_done"), sem("hl_done")
        vec_mm, vec_done, f_mm, f_step, f_sin = sem("vec_mm"), sem("vec_done"), sem("f_mm"), sem("f_step"), sem("f_sin")
        f_clamp, x_mm, pv_mm = sem("f_clamp"), sem("x_mm"), sem("pv_mm")
        dec_done, filt_mm, filt_done = sem("dec_done"), sem("filt_mm"), sem("filt_done")
        conv_done, tap_done, u_done, ut_mm, ut_done = (sem("conv_done"), sem("tap_done"), sem("u_done"), sem("ut_mm"),
                                                       sem("ut_done"))
        pad_done, win_step, pooled = sem("pad_done"), sem("win_step"), sem("pooled")
        kf_mm, kf_done, u_mm, prod_done, spec_done = (sem("kf_mm"), sem("kf_done"), sem("u_mm"), sem("prod_done"),
                                                      sem("spec_done"))
        mix_mm, inv_mm, gated, ah_done, al_done = (sem("mix_mm"), sem("inv_mm"), sem("gated"), sem("ah_done"),
                                                   sem("al_done"))
        s_mm, s_used, mx_done, exp_done, rs_done, p_done = (sem("s_mm"), sem("s_used"), sem("mx_done"), sem("exp_done"),
                                                            sem("rs_done"), sem("p_done"))
        t_mm, t_done, oh_done, ol_done = sem("t_mm"), sem("t_done"), sem("oh_done"), sem("ol_done")
        sqq_done, sqk_done, ms_mm, ms_std, kw_done = (sem("sqq_done"), sem("sqk_done"), sem("ms_mm"), sem("ms_std"),
                                                      sem("kw_done"))
        rqk_done = sem("rqk_done")
        kb_mm, kn_done, qs_done, v_mm, vs_done = (sem("kb_mm"), sem("kn_done"), sem("qs_done"), sem("v_mm"),
                                                  sem("vs_done"))
        mask_done, gqk_done, y_ready, y_mm, y_copied = (sem("mask_done"), sem("gqk_done"), sem("y_ready"), sem("y_mm"),
                                                        sem("y_copied"))
        y_out = [sem(f"y_out{s}") for s in range(2)]

        block = ctx.enter_context(nc.Block())

        def settle(eng):
            eng.wait_ge(low, LOW_CREDIT)

        def unit_source(ph, i, j):
            if ph.name.startswith("up"):
                return (wu if j % 2 else wg)[ffn_of[ph.name], :, :, bass.ds((2 * i + j // 2) * P, P)]
            if ph.name.startswith("down"):
                return wd[ffn_of[ph.name], :, (j % 2) * (KF // 2):(j % 2 + 1) * (KF // 2),
                          bass.ds((2 * i + j // 2) * P, P)]
            if ph.name == "w_in":
                return w_in[:, :, bass.ds((3 - j) * HW + i * P, P)]
            if ph.name == "qkv":
                return w_qkv[:, :, bass.ds(j * D + i * P, P)]
            return (w_out if ph.name == "w_out" else w_o)[:, :, bass.ds((4 * i + j) * P, P)]

        @block.sync
        def _(sp):
            for t in range(TT):
                sp.dma_start(xrow[:, t, :], (a["x_prompt"] if t < 2 else a["x_sample"])[0, (t % 2) * P:(t % 2 + 1) * P, :])\
                  .then_inc(x_in[t], 16)

            def load(ph, i):
                for j in range(ph.per):
                    sp.wait_ge(low, ph.unit(i, j) - 2 + LOW_CREDIT)
                    sp.dma_start(raw[j][:, 0:ph.kt, :], unit_source(ph, i, j)).then_inc(raw_in[j], 16)

            for ph in phases:
                if ph.name == "w_in":
                    for i in range(ph.iters):
                        load(ph, i)
                else:
                    with sp.Fori(0, ph.iters) as i:
                        load(ph, i)

        def split_place(ph, j):
            return (j if ph.name == "qkv" else j % 2), j

        def ahead(ph, i, j, last):
            if j + 2 < ph.per:
                return ph, i, j + 2
            if last:
                return (ph.next, 0, j + 2 - ph.per) if ph.next else (None, 0, 0)
            return ph, i + 1, j + 2 - ph.per

        def split_high(act, ph, i, j):
            if ph is None:
                return
            w, r = split_place(ph, j)
            act.wait_ge(raw_in[r], 16 * (ph.uses0[r] + 1 + i))
            act.wait_ge(unit_done, ph.unit(i, j) - 1 + UNIT_CREDIT)
            act.activation(wh[w][:, 0:ph.kt, :], raw[r][:, 0:ph.kt, :], ACT.Copy).then_inc(high, 1)

        def split_low(dve, ph, i, j):
            if ph is None:
                return
            w, r = split_place(ph, j)
            dve.wait_ge(high, ph.unit(i, j) + 1)
            dve.tensor_tensor(wl[w][:, 0:ph.kt, :], raw[r][:, 0:ph.kt, :], wh[w][:, 0:ph.kt, :].bitcast(F32),
                              ALU.subtract).then_inc(low, 1)

        def chunk_base(norm):
            return KD * norm

        def out_chunk(ph, i, j):
            return 2 * i + j // 2 if ph.name.startswith("down") else 4 * i + j

        def phase_loop(eng, ph, body, after_first=None):
            first = 0
            if after_first:
                body(0, False)
                after_first()
                first = 1
            if ph.iters - 1 > first:
                with eng.Fori(first, ph.iters - 1) as i:
                    body(i, False)
            body(ph.iters - 1, True)

        @block.scalar
        def _(act):
            col = lambda n: vec[:, bass.ds(n, 1)]

            act.dma_start(cst[:, :], a["c_small"]).then_inc(const_in, 16)
            rows = [(V_NORM, a["norm_g"].rearrange("l n (k p) -> (l n k) p", p=P)),
                    (V_PSCALE, a["pool_scale"].rearrange("o (k p) -> (o k) p", p=P)),
                    (V_SW, a["short_w"].rearrange("o n (k p) -> (o n k) p", p=P)),
                    (V_SB, a["short_b"].rearrange("o (k p) -> (o k) p", p=P))]
            for n, (at, src) in enumerate(rows):
                act.dma_start(vrow[at:at + src.shape[0], :], src).then_inc(vec_in, 16)
            for at, name in ((V_GQ, "q_norm_g"), (V_GK, "k_norm_g"), (V_B1, "filt_b1"), (V_B1 + 1, "filt_b2"),
                             (V_B1 + 2, "filt_b3"), (V_FREQ, "filt_freq")):
                for half in range(2):
                    act.dma_start(vrow[at:at + 1, half * HD:(half + 1) * HD], a[name]).then_inc(vec_in, 16)
            act.dma_start(zT[:, :], a["c_z"]).then_inc(filt_in, 16)
            act.dma_start(fw1[:, :], a["filt_w1"][0]).then_inc(filt_in, 16)
            act.dma_start(fw2[:, :], a["filt_w2"][0]).then_inc(filt_in, 16)
            act.dma_start(fw3[:, :], a["filt_w3"][0]).then_inc(filt_in, 16)

            def residual(ph, i, j, norm):
                d = out_chunk(ph, i, j)
                act.wait_ge(evac, ph.group(i, j) + 1 + EVAC_CREDIT)
                settle(act)
                residual_parts(norm, d, j // 2 % 2 if ph.name.startswith("down") else j % 2)

            def residual_parts(norm, d, parity):
                act.activation(xh[:, bass.ds(d, 1), :], x[:, bass.ds(d, 1), :], ACT.Copy,
                               scale=col(V_NORM + norm * KD + d)).then_inc(xh_done, 1)
                act.activation(sqtmp[:, parity, :], x[:, bass.ds(d, 1), :], ACT.Square).then_inc(sq_done, 1)

            def norm_std(norm):
                act.wait_ge(mean_mm, norm + 1)
                act.activation(rcol[:, :], bank[7][:, 0:TT], ACT.Sqrt, bias=cst[:, C_EPS:C_EPS + 1]).then_inc(std_done, 1)

            def evacuate(ph, i, j):
                if ph.name.startswith("up"):
                    f = 2 * i + j // 2
                    g, u = ga[j // 2], ua[j // 2]
                    if j % 2 == 0:
                        act.wait_ge(evac, ph.group(i, j) + 1 + EVAC_CREDIT)
                        act.activation(g[:, :], g[:, :], ACT.Silu).then_inc(silu_done, 1)
                    else:
                        act.wait_ge(h_done, KF * ffn_of[ph.name] + f + 1)
                        settle(act)
                        act.activation(hh[:, bass.ds(f, 1), :], u[:, :], ACT.Copy).then_inc(hh_done, 1)
                elif ph.name in NEXT_NORM:
                    if j in ph.groups_at:
                        residual(ph, i, j, NEXT_NORM[ph.name])
                elif ph.name == "down3":
                    if j in ph.groups_at:
                        s, d = j // 2, out_chunk(ph, i, j)
                        act.wait_ge(y_mm, d + 1)
                        act.wait_ge(y_out[s], 32 * i + STORE_CREDIT)
                        act.activation(ua[s][:, :], bank[2 + s][:, :], ACT.Copy).then_inc(y_copied, 1)
                        act.wait_ge(y_copied, d + 1 + COPY_CREDIT)
                        for n, y in enumerate((y_prompt, y_sample)):
                            act.dma_start(y[0].rearrange("(t p) c -> p t c", p=P)[:, :, bass.ds(d * P, P)],
                                          ua[s][:, n * SEQ:(n + 1) * SEQ].rearrange("p (t c) -> p t c", t=2))\
                               .then_inc(y_out[s], 16)
                elif ph.name == "w_in":
                    if j < 3:
                        at = (2 - j) * KH + i
                        dst = x0[:, bass.ds(i, 1), :] if j == 2 else ua[j][:, :]
                        act.wait_ge(evac, ph.group(i, j) + 1 + EVAC_CREDIT)
                        settle(act)
                        act.activation(dst, ga[j % 2][:, :], ACT.Identity, bias=col(V_SB + at),
                                       scale=col(V_SW + 3 * KH + at)).then_inc(conv_done, 1)
                    else:
                        act.wait_ge(ut_mm, i + 1)
                        settle(act)
                        act.activation(ut[:, :, bass.ds(i * P, P)], bank[2][:, :].rearrange("p (t c) -> p t c", t=TT),
                                       ACT.Copy).then_inc(ut_done, 1)

            for n in range(3):
                act.wait_ge(f_step, 6 * (n + 1))
                act.activation((fh if n < 2 else h3)[:, :], fa[:, :], ACT.Sin).then_inc(f_sin, 1)
            for d in range(KD):
                act.wait_ge(evac, d + 1 + EVAC_CREDIT)
                residual_parts(0, d, d % 2)
            for j in range(2):
                split_high(act, phases[0], 0, j)
            for r in range(DR):
                src = bass.AP(a["rpb"].tensor, (RPB_R // 2 - ROWS + 1 + r) * RPB_C + RPB_C // 2,
                              [[RPB_R * RPB_C, HEADS], [-1, GRID_W], [1, GRID_W]])
                act.dma_start(bias_dram[:, :, r * GRID_W:(r + 1) * GRID_W].rearrange("q h c -> h q c"), src)\
                   .then_inc(toep_in, 16)

            def attention(p, projects, attends, last):
                ph = by["qkv"]
                if projects:
                    if attends:
                        act.wait_ge(mask_done, p)
                    else:
                        act.wait_ge(toep_in, 16 * DR)
                    for half in range(2):
                        act.dma_start(braw[half * HD:(half + 1) * HD, :, :],
                                      bias_dram[:, bass.ds(2 * p, 2), (1 - half) * GRID_W:(7 - half) * GRID_W])\
                           .then_inc(braw_in, 16)
                    split_high(act, *ahead(ph, p, 0, last))
                    act.wait_ge(evac, ph.group(p, 0) + 1 + EVAC_CREDIT)
                    act.activation(sqq[:, :], qt[:, :], ACT.Square).then_inc(sqq_done, 1)

                def exps(h):
                    n = 4 * (p - 1) + h
                    act.wait_ge(mx_done, n + 1)
                    for t in range(2):
                        act.activation(sc[:, h % 2, t, :], sc[:, h % 2, t, :], ACT.Exp, bias=nmax[:, h % 2, t:t + 1],
                                       accum_out=rsum[:, h % 2, t:t + 1]).then_inc(exp_done, 1)

                def probs_t(h):
                    n = 4 * (p - 1) + h
                    act.wait_ge(t_mm, n + 1)
                    act.wait_ge(pv_mm, n - 1 + VALUE_CREDIT)
                    act.activation(pt[:, h % 2, :, :], bank[6][:, :].rearrange("p (k q) -> p k q", k=2), ACT.Copy)\
                       .then_inc(t_done, 1)

                if attends:
                    exps(0)
                    exps(1)
                if projects:
                    split_high(act, *ahead(ph, p, 1, last))
                    act.wait_ge(evac, ph.group(p, 1) + 1 + EVAC_CREDIT)
                    act.activation(sqk[:, :], kt[:, :], ACT.Square).then_inc(sqk_done, 1)
                if attends:
                    probs_t(0)
                    exps(2)
                    probs_t(1)
                    exps(3)
                if projects:
                    act.wait_ge(ms_mm, p + 1)
                    act.activation(rqk[:, :, :, :], bank[3][:, 0:4 * TT].rearrange("p (a t h) -> p a t h", a=2, t=TT),
                                   ACT.Sqrt, bias=cst[:, C_EPS:C_EPS + 1]).then_inc(ms_std, 1)
                    if attends:
                        act.wait_ge(s_mm, 4 * p)
                    act.activation(qs[:, :], qt[:, :], ACT.Copy, scale=gqk[:, 0:1]).then_inc(qs_done, 1)
                    split_high(act, *ahead(ph, p, 2, last))
                if attends:
                    probs_t(2)
                    probs_t(3)
                if projects:
                    act.wait_ge(v_mm, p + 1)
                    if attends:
                        act.wait_ge(pv_mm, 4 * p + VALUE_CREDIT)
                    act.activation(vs[:, :, :], bank[3][:, :].rearrange("p (t c) -> p t c", t=TT), ACT.Copy)\
                       .then_inc(vs_done, 1)
                if attends:
                    act.wait_ge(pv_mm, 4 * p + VALUE_CREDIT)
                    settle(act)
                    act.activation(oh[:, bass.ds(p - 1, 1), :], bank[7][:, :], ACT.Copy).then_inc(oh_done, 1)

            for ph in phases:
                if ph.name == "w_in":
                    act.wait_ge(unit_done, ph.unit0 + UNIT_CREDIT)
                    act.dma_start(absd[:, :], a["filt_deltas"].to_broadcast([P, 2 * HW])).then_inc(mix_in, 16)
                    act.dma_start(fwo[:, :], a["filt_w_out"][0]).then_inc(mix_in, 16)
                    act.dma_start(hbias[:, :], a["hyena_bias"]).then_inc(mix_in, 16)
                    act.dma_start(poolw[:, :, :], a["pool_w"][0].rearrange("g c d -> c g d")).then_inc(mix_in, 16)
                    act.dma_start(dft[:, :, :, :], a["c_dft"][:, 0]).then_inc(mix_in, 16)
                    act.dma_start(idft[:, :, :], a["c_dft"][:, 1].rearrange("p a b m -> p (a b) m")).then_inc(mix_in, 16)
                    act.dma_start(icnt[:, :, :], a["c_dft"][:, 2].rearrange("p a b m -> p (a b) m")).then_inc(mix_in, 16)
                if ph.name in NORM_OF:
                    norm_std(NORM_OF[ph.name])
                if ph.name == "qkv":
                    attention(0, True, False, False)
                    with act.Fori(1, PAIRS - 1) as p:
                        attention(p, True, True, False)
                    attention(PAIRS - 1, True, True, True)
                    attention(PAIRS, False, True, False)
                    continue

                def body(i, last, ph=ph):
                    for j in range(ph.per):
                        if last and ph.next:
                            evacuate(ph, i, j)
                        split_high(act, *ahead(ph, i, j, last))
                        if not last or not ph.next:
                            evacuate(ph, i, j)

                def decays():
                    act.wait_ge(mix_in, 16 * 7)
                    act.activation(absd[:, :], absd[:, :], ACT.Abs).then_inc(dec_done, 1)
                    act.wait_ge(dec_done, 1)
                    for t in range(2):
                        act.activation(decay[:, t, :, :].rearrange("p a c -> p (a c)"), absd[:, :], ACT.Exp,
                                       scale=cst[:, C_T + t:C_T + t + 1]).then_inc(dec_done, 1)

                phase_loop(act, ph, body, after_first=decays if ph.name == "w_in" else None)
                if ph.name == "w_in":
                    for n in range(4):
                        act.wait_ge(kf_mm, n + 1)
                        act.activation(kf[:, n // 2, n % 2, :], bank[3 + n][:, :], ACT.Copy).then_inc(kf_done, 1)
                    for g in range(4):
                        act.wait_ge(mix_mm, g + 1)
                        act.activation(ah[:, g, :], bank[7 if g % 2 else 2][:, :], ACT.Copy,
                                       scale=col(V_PSCALE + g)).then_inc(ah_done, 1)
                    for c in range(KH):
                        act.wait_ge(gated, c + 1)
                        act.activation(ah[:, 4 + c, :], x0[:, c, :], ACT.Copy).then_inc(ah_done, 1)
            for s in range(2):
                act.wait_ge(y_out[s], 16 * KD + STORE_CREDIT)

        @block.vector
        def _(dve):
            col = lambda n, rows=P: vec[0:rows, bass.ds(n, 1)]

            dve.memset(sqacc[:, :], 0.0).then_inc(low, LOW_CREDIT)
            for n, (s, credit) in enumerate(((unit_done, UNIT_CREDIT), (evac, EVAC_CREDIT), (s_used, SCORE_CREDIT),
                                             (t_done, TURN_CREDIT), (pv_mm, VALUE_CREDIT), (ol_done, OUT_CREDIT),
                                             (y_copied, COPY_CREDIT), (y_out[0], STORE_CREDIT), (y_out[1], STORE_CREDIT))):
                dve.memset(sqtmp[:, 0, n:n + 1], 0.0).then_inc(s, credit)
            dve.wait_ge(low, LOW_CREDIT)
            dve.wait_ge(vec_mm, 1)
            dve.tensor_copy(vec[:, :], bank[7][:, 0:V_ALL]).then_inc(vec_done, 1)
            dve.wait_ge(vec_done, 1)
            dve.scalar_tensor_tensor(out=gqk[:, :], in0=vec[:, V_GQ:V_GQ + 1], scalar=HD ** -0.5,
                                     in1=vec[:, V_GK:V_GK + 1], op0=ALU.mult, op1=ALU.mult).then_inc(gqk_done, 1)

            def filter_layer(n):
                s = 6 * n
                dve.wait_ge(f_mm, n + 1)
                dve.tensor_scalar(fa[:, :], bank[6][0:HID, 0:SEQ], col(V_B1 + n, HID), col(V_FREQ, HID),
                                  ALU.add, ALU.mult).then_inc(f_step, 1)
                dve.wait_ge(f_step, s + 1)
                dve.tensor_scalar(fk[:, :], fa[:, :], 1.0 / TWO_PI, MAGIC, ALU.mult, ALU.add).then_inc(f_step, 1)
                dve.wait_ge(f_step, s + 2)
                dve.tensor_scalar(fk[:, :], fk[:, :], MAGIC, None, ALU.subtract).then_inc(f_step, 1)
                for m, part in enumerate((PI_A, PI_B, PI_C)):
                    dve.wait_ge(f_step, s + 3 + m)
                    ins = dve.scalar_tensor_tensor(out=fa[:, :], in0=fk[:, :], scalar=-part, in1=fa[:, :],
                                                   op0=ALU.mult, op1=ALU.add)
                    if m < 2:
                        ins.then_inc(f_step, 1)
                    else:
                        ins.then_inc(f_clamp, 1)
                dve.wait_ge(f_clamp, n + 1)
                dve.tensor_scalar(fa[:, :], fa[:, :], SIN_MAX, -SIN_MAX, ALU.min, ALU.max).then_inc(f_step, 1)

            def residual_low(norm, d, parity):
                dve.wait_ge(xh_done, chunk_base(norm) + d + 1)
                dve.scalar_tensor_tensor(out=xl[:, bass.ds(d, 1), :], in0=x[:, bass.ds(d, 1), :],
                                         scalar=col(V_NORM + norm * KD + d), in1=xh[:, bass.ds(d, 1), :].bitcast(F32),
                                         op0=ALU.mult, op1=ALU.subtract).then_inc(xl_done, 1)
                dve.wait_ge(sq_done, chunk_base(norm) + d + 1)
                dve.wait_ge(acc_done, chunk_base(norm) + d) if not (isinstance(d, int) and norm == 0 and d == 0) else None
                dve.tensor_tensor(sqacc[:, :], sqacc[:, :], sqtmp[:, parity, :], ALU.add).then_inc(acc_done, 1)

            def norm_factor(norm):
                dve.wait_ge(std_done, norm + 1)
                dve.reciprocal(rcol[:, :], rcol[:, :]).then_inc(rwide_done, 1)
                dve.wait_ge(rwide_done, 2 * norm + 1)
                dve.tensor_copy(rwide[:, :, :], rcol[:, :].unsqueeze(2).to_broadcast([P, TT, P])).then_inc(rwide_done, 1)
                dve.wait_ge(rbc_mm, norm + 1)
                dve.tensor_copy(rbc[:, :], bank[7][:, :]).then_inc(rbc_done, 1)
                dve.memset(sqacc[:, :], 0.0).then_inc(rbc_done, 1)
                dve.wait_ge(rbc_done, 2 * norm + 2)

            def scaled(ph, i, j, out, b, shape=None):
                dve.wait_ge(unit_done, ph.unit(i, j) + 1 + UNIT_CREDIT)
                src, r = bank[b][:, :], rbc[:, :]
                if shape:
                    src, r = src.rearrange(shape, s=NSEQ), r.rearrange(shape, s=NSEQ)
                dve.tensor_tensor(out, src, r, ALU.mult).then_inc(evac, 1)

            def evacuate(ph, i, j):
                if ph.name.startswith("up"):
                    n, f = KF * ffn_of[ph.name], 2 * i + j // 2
                    g, u = ga[j // 2], ua[j // 2]
                    scaled(ph, i, j, (u if j % 2 else g)[:, :], j % 2)
                    if j % 2:
                        dve.wait_ge(silu_done, n + f + 1)
                        dve.wait_ge(evac, ph.group(i, j) + 1 + EVAC_CREDIT)
                        dve.tensor_tensor(u[:, :], g[:, :], u[:, :], ALU.mult).then_inc(h_done, 1)
                        dve.wait_ge(hh_done, n + f + 1)
                        dve.tensor_tensor(hl[:, bass.ds(f, 1), :], u[:, :], hh[:, bass.ds(f, 1), :].bitcast(F32),
                                          ALU.subtract).then_inc(hl_done, 1)
                elif ph.name == "w_in":
                    if j == 3:
                        scaled(ph, i, j, ppad[:, bass.ds(i, 1), :, PAD:PAD + SEQ].rearrange("p o s t -> p (o s) t"), 1,
                               "p (s t) -> p s t")
                        return
                    n = 3 * i + j
                    src = ga[j % 2]
                    if not isinstance(n, int) or n > 0:
                        dve.wait_ge(tap_done, 2 * n)
                    scaled(ph, i, j, src[:, :], j % 2)
                    dst = x0[:, bass.ds(i, 1), :] if j == 2 else ua[j][:, :]
                    dst = dst.rearrange("p o (s t) -> p (o s) t", s=NSEQ) if j == 2 else dst.rearrange("p (s t) -> p s t", s=NSEQ)
                    src = src[:, :].rearrange("p (s t) -> p s t", s=NSEQ)
                    at = (2 - j) * KH + i
                    dve.wait_ge(conv_done, n + 1)
                    dve.scalar_tensor_tensor(out=dst[:, :, 1:SEQ], in0=src[:, :, 0:SEQ - 1], scalar=col(V_SW + at),
                                             in1=dst[:, :, 1:SEQ], op0=ALU.mult, op1=ALU.add).then_inc(tap_done, 1)
                    dve.wait_ge(tap_done, 2 * n + 1)
                    dve.scalar_tensor_tensor(out=dst[:, :, 0:SEQ - 1], in0=src[:, :, 1:SEQ],
                                             scalar=col(V_SW + 6 * KH + at), in1=dst[:, :, 0:SEQ - 1],
                                             op0=ALU.mult, op1=ALU.add).then_inc(tap_done, 1)
                    if j == 1:
                        dve.wait_ge(tap_done, 2 * n + 2)
                        dve.tensor_tensor(up[:, :], ua[0][:, :], ua[1][:, :], ALU.mult).then_inc(u_done, 1)
                elif j in ph.groups_at:
                    d = out_chunk(ph, i, j)
                    parity = j // 2 % 2 if ph.name.startswith("down") else j % 2
                    factor = 0.5 if ph.name.startswith("down") else 1.0
                    b = parity
                    dve.wait_ge(unit_done, ph.unit(i, j) + 1 + UNIT_CREDIT)
                    out = ga[parity][:, :] if ph.name == "down3" else x[:, bass.ds(d, 1), :]
                    dve.scalar_tensor_tensor(out=out, in0=bank[b][:, :], scalar=factor, in1=x[:, bass.ds(d, 1), :],
                                             op0=ALU.mult, op1=ALU.add).then_inc(evac, 1)
                    if ph.name != "down3":
                        residual_low(NEXT_NORM[ph.name], d, parity)

            for n in range(3):
                filter_layer(n)
            for d in range(KD):
                dve.wait_ge(x_mm, d + 1)
                dve.tensor_copy(x[:, d, :], bank[d % 2][:, :]).then_inc(evac, 1)
                residual_low(0, d, d % 2)
            for j in range(2):
                split_low(dve, phases[0], 0, j)

            def attention(p, projects, attends, last):
                ph = by["qkv"]

                def maxima(h):
                    s, a_ = h // 2, h % 2
                    n = 4 * (p - 1) + h
                    dve.wait_ge(s_mm, n + 1)
                    for t in range(2):
                        dve.scalar_tensor_tensor(out=sc[:, h % 2, t, :], in0=bank[4 + h % 2][:, t * SEQ:(t + 1) * SEQ],
                                                 scalar=rqk[:, 0, 2 * s + t, a_:a_ + 1],
                                                 in1=bmask[:, a_, (2 - 2 * t) * GRID_W:(6 - 2 * t) * GRID_W],
                                                 op0=ALU.mult, op1=ALU.add).then_inc(s_used, 1)
                    dve.wait_ge(s_used, 2 * (n + 1) + SCORE_CREDIT)
                    dve.tensor_reduce(nmax[:, h % 2, :], sc[:, h % 2, :, :], AX.X, ALU.max, negate=True)\
                       .then_inc(mx_done, 1)

                def normalise(h):
                    n = 4 * (p - 1) + h
                    dve.wait_ge(exp_done, 2 * n + 2)
                    dve.reciprocal(rsum[:, h % 2, :], rsum[:, h % 2, :]).then_inc(rs_done, 1)
                    dve.wait_ge(rs_done, n + 1)
                    for t in range(2):
                        dve.tensor_scalar(sc[:, h % 2, t, :], sc[:, h % 2, t, :], rsum[:, h % 2, t:t + 1], None,
                                          ALU.mult).then_inc(p_done, 1)

                if projects:
                    if attends:
                        dve.wait_ge(qs_done, p)
                    scaled(ph, p, 0, qt[:, :], 0)
                    split_low(dve, *ahead(ph, p, 0, last))
                if attends:
                    dve.wait_ge(mask_done, p)
                    maxima(0)
                    maxima(1)
                    normalise(0)
                    normalise(1)
                if projects:
                    scaled(ph, p, 1, kt[:, :], 1)
                    split_low(dve, *ahead(ph, p, 1, last))
                if attends:
                    maxima(2)
                    maxima(3)
                    normalise(2)
                    normalise(3)
                if projects:
                    dve.wait_ge(ms_std, p + 1)
                    dve.reciprocal(rqk[:, :, :, :], rqk[:, :, :, :]).then_inc(rqk_done, 1)
                    dve.wait_ge(rqk_done, p + 1)
                    dve.tensor_copy(kwide[:, :, :].rearrange("p t (h c) -> p t h c", h=2),
                                    rqk[:, 1, :, :].unsqueeze(3).to_broadcast([P, TT, 2, HD])).then_inc(kw_done, 1)
                    dve.wait_ge(kb_mm, p + 1)
                    if attends:
                        dve.wait_ge(s_mm, 4 * p)
                    dve.tensor_tensor(kn[:, :], kt[:, :], bank[3][:, :], ALU.mult).then_inc(kn_done, 1)
                    if attends:
                        dve.wait_ge(v_mm, p)
                    scaled(ph, p, 2, vt[:, :], 2)
                    split_low(dve, *ahead(ph, p, 2, last))
                if attends:
                    dve.wait_ge(oh_done, p)
                    dve.tensor_tensor(ol[:, bass.ds(p - 1, 1), :], bank[7][:, :],
                                      oh[:, bass.ds(p - 1, 1), :].bitcast(F32), ALU.subtract).then_inc(ol_done, 1)

            for ph in phases:
                if ph.name == "w_in":
                    dve.wait_ge(pad_done, 1)
                if ph.name in NORM_OF:
                    norm_factor(NORM_OF[ph.name])
                if ph.name == "qkv":
                    attention(0, True, False, False)
                    with dve.Fori(1, PAIRS - 1) as p:
                        attention(p, True, True, False)
                    attention(PAIRS - 1, True, True, True)
                    attention(PAIRS, False, True, False)
                    continue

                def body(i, last, ph=ph):
                    for j in range(ph.per):
                        if last and ph.next:
                            evacuate(ph, i, j)
                        split_low(dve, *ahead(ph, i, j, last))
                        if not last or not ph.next:
                            evacuate(ph, i, j)

                def filter_in_time():
                    for t in range(2):
                        for half in range(2):
                            n = 2 * t + half
                            dve.wait_ge(filt_mm, n + 1)
                            dve.wait_ge(dec_done, 2 + t)
                            dve.scalar_tensor_tensor(out=filt[:, t, half, :], in0=decay[:, t, half, :], scalar=0.05,
                                                     in1=bank[3 + n][:, :], op0=ALU.add, op1=ALU.mult)\
                               .then_inc(filt_done, 1)
                    dve.wait_ge(filt_done, 4)
                    dve.memset(filt[0:1, 0, 1, :], 0.0).then_inc(filt_done, 1)
                    dve.wait_ge(filt_done, 5)
                    dve.tensor_tensor(hsum[:, :, :], filt[:, :, 0, :], filt[:, :, 1, :], ALU.add).then_inc(filt_done, 1)
                    dve.tensor_tensor(hdif[:, :, :], filt[:, :, 0, :], filt[:, :, 1, :], ALU.subtract)\
                       .then_inc(filt_done, 1)
                    dve.wait_ge(filt_done, 7)
                    dve.tensor_tensor(hsum[0:1, 0, :], hsum[0:1, 0, :], hbias[:, :], ALU.add).then_inc(filt_done, 1)

                phase_loop(dve, ph, body, after_first=filter_in_time if ph.name == "w_in" else None)
                if ph.name == "w_in":
                    dve.wait_ge(kf_done, 4)
                    dve.wait_ge(tap_done, 6 * KH)
                    for n in range(4):
                        s, m = n // 2, n % 2
                        part = [ga[0], ua[0]] if n % 2 == 0 else [ga[1], ua[1]]
                        if n >= 2:
                            dve.wait_ge(spec_done, 2 * (n - 1))
                        for cs in range(2):
                            dve.wait_ge(u_mm, 2 * n + cs + 1)
                            b = bank[3 + 2 * (n % 2) + cs]
                            for k in range(2):
                                out = spec[:, s, k, m, :] if cs == 0 else part[k][:, :]
                                dve.tensor_tensor(out, b[:, :], kf[:, k if cs == 0 else 1 - k, m, :], ALU.mult)\
                                   .then_inc(prod_done, 1)
                    for g in range(4):
                        dve.wait_ge(ah_done, g + 1)
                        dve.scalar_tensor_tensor(out=al[:, g, :], in0=bank[7 if g % 2 else 2][:, :],
                                                 scalar=col(V_PSCALE + g), in1=ah[:, g, :].bitcast(F32),
                                                 op0=ALU.mult, op1=ALU.subtract).then_inc(al_done, 1)
                    for c in range(KH):
                        dve.wait_ge(inv_mm, c + 1)
                        dve.tensor_tensor(x0[:, c, :], bank[3 + c][:, :], x0[:, c, :], ALU.mult).then_inc(gated, 1)
                        dve.wait_ge(ah_done, 4 + c + 1)
                        dve.tensor_tensor(al[:, 4 + c, :], x0[:, c, :], ah[:, 4 + c, :].bitcast(F32), ALU.subtract)\
                           .then_inc(al_done, 1)

        @block.tensor
        def _(pe):
            def three(out, w, k, b, hi, lo, at, start, stop):
                pe.matmul(out, wh[w][:, k, :], hi[:, at, :], start=start, stop=False)
                pe.matmul(out, wh[w][:, k, :], lo[:, at, :], start=False, stop=False)
                return pe.matmul(out, wl[w][:, k, :], hi[:, at, :], start=False, stop=stop)

            def unit(ph, i, j, waits=None, hook=None):
                w = split_place(ph, j)[0]
                half = ph.name.startswith("down")
                first = not half or j % 2 == 0
                ends = j in ph.groups_at
                hi, lo = ((hh, hl) if half else (ah, al) if ph.name == "w_out" else (oh, ol) if ph.name == "w_o"
                          else (xh, xl))
                b = j if ph.name == "qkv" else (j // 2 if half else j % 2)
                pe.wait_ge(low, ph.unit(i, j) + 1 + LOW_CREDIT)
                if first:
                    g = ph.group(i, ph.groups_at[0] if half and j < 2 else ph.groups_at[1] if half else j)
                    pe.wait_ge(evac, g - 1 + EVAC_CREDIT)
                for k in range(ph.kt):
                    if waits and waits[k]:
                        pe.wait_ge(*waits[k])
                    if hook and k == 5:
                        hook()
                    last = three(bank[b][:, :], w, k, b, hi, lo, k + (KF // 2 if half and j % 2 else 0),
                                 start=first and k == 0, stop=ends and k == ph.kt - 1)
                last.then_inc(unit_done, 1)

            def norm_mean(norm):
                pe.wait_ge(acc_done, chunk_base(norm) + KD)
                for t in range(TT):
                    last = pe.matmul(bank[7][:, t:t + 1], sqacc[:, t * P:(t + 1) * P], cst[:, C_MEAN:C_MEAN + 1],
                                     start=True, stop=True)
                last.then_inc(mean_mm, 1)

            def norm_spread(norm):
                pe.wait_ge(rwide_done, 2 * norm + 2)
                for t in range(TT):
                    last = pe.matmul(bank[7][:, t * P:(t + 1) * P], rwide[:, t, :], ident, start=True, stop=True)
                last.then_inc(rbc_mm, 1)

            pe.wait_ge(const_in, 16)
            pe.wait_ge(vec_in, 16 * 16)
            pe.transpose(bank[7][:, 0:V_ALL], vrow[:, :], cst[0:V_ALL, C_ID:C_ID + V_ALL]).then_inc(vec_mm, 1)
            pe.wait_ge(filt_in, 64)
            for n in range(3):
                w, z = ((fw1, zT), (fw2, fh), (fw3, fh))[n]
                if n:
                    pe.wait_ge(f_sin, n)
                pe.matmul(bank[6][0:HID, 0:SEQ], w[:, :], z[:, :], start=True, stop=True).then_inc(f_mm, 1)
            for d in range(KD):
                for t in range(TT):
                    if d == 0:
                        pe.wait_ge(x_in[t], 16)
                    elif t == 0 and d >= 2:
                        pe.wait_ge(evac, d - 1 + EVAC_CREDIT)
                    last = pe.transpose(bank[d % 2][:, t * P:(t + 1) * P], xrow[:, t, d * P:(d + 1) * P], ident)
                last.then_inc(x_mm, 1)

            def turn_u(i):
                pe.wait_ge(u_done, i + 1)
                if not isinstance(i, int) or i > 0:
                    pe.wait_ge(ut_done, i)
                for t in range(TT):
                    last = pe.transpose(bank[2][:, t * P:(t + 1) * P], up[:, t * P:(t + 1) * P], ident)
                last.then_inc(ut_mm, 1)

            def turn_y(d, s):
                pe.wait_ge(evac, by["down3"].group0 + d + 1 + EVAC_CREDIT)
                pe.wait_ge(y_copied, d - 1 + COPY_CREDIT)
                for t in range(TT):
                    last = pe.transpose(bank[2 + s][:, t * P:(t + 1) * P], ga[s][:, t * P:(t + 1) * P], ident)
                last.then_inc(y_mm, 1)

            def attention(p, projects, attends, last_one):
                ph = by["qkv"]

                def scores(h):
                    s, a_ = h // 2, h % 2
                    n = 4 * (p - 1) + h
                    pe.wait_ge(s_used, 2 * (n - 1) + SCORE_CREDIT)
                    for t in range(2):
                        at = s * SEQ + t * P
                        last = pe.matmul(bank[4 + h % 2][:, t * SEQ:(t + 1) * SEQ], qs[a_ * HD:(a_ + 1) * HD, at:at + P],
                                         kn[a_ * HD:(a_ + 1) * HD, s * SEQ:(s + 1) * SEQ], start=True, stop=True)
                    last.then_inc(s_mm, 1)

                def turn(h):
                    n = 4 * (p - 1) + h
                    pe.wait_ge(p_done, 2 * n + 2)
                    pe.wait_ge(t_done, n + TURN_CREDIT)
                    for k in range(2):
                        for t in range(2):
                            last = pe.transpose(bank[6][:, k * SEQ + t * P:k * SEQ + (t + 1) * P],
                                                sc[:, h % 2, t, k * P:(k + 1) * P], ident)
                    last.then_inc(t_mm, 1)

                def values(h):
                    s, a_ = h // 2, h % 2
                    n = 4 * (p - 1) + h
                    pe.wait_ge(t_done, n + 1 + TURN_CREDIT)
                    for k in range(2):
                        last = pe.matmul(bank[7][a_ * HD:(a_ + 1) * HD, s * SEQ:(s + 1) * SEQ],
                                         vs[:, 2 * s + k, a_ * HD:(a_ + 1) * HD], pt[:, h % 2, k, :],
                                         start=(k == 0), stop=(k == 1))
                    last.then_inc(pv_mm, 1)

                if projects:
                    if attends:
                        unit(ph, p, 0)
                    else:
                        unit(ph, 0, 0, waits=[(xl_done, chunk_base(4) + k + 1) for k in range(KD)])
                        norm_mean(4)
                if attends:
                    pe.wait_ge(kn_done, p)
                    pe.wait_ge(qs_done, p)
                    scores(0)
                    scores(1)
                if projects:
                    unit(ph, p, 1, hook=None if attends else lambda: norm_spread(4))
                if attends:
                    turn(0)
                    scores(2)
                    pe.wait_ge(vs_done, p)
                    pe.wait_ge(ol_done, p - 1 + OUT_CREDIT)
                    values(0)
                    turn(1)
                    scores(3)
                if projects:
                    pe.wait_ge(sqq_done, p + 1)
                    pe.wait_ge(sqk_done, p + 1)
                    if attends:
                        pe.wait_ge(vs_done, p)
                    for a_, sq in enumerate((sqq, sqk)):
                        for t in range(TT):
                            at = a_ * 2 * TT + 2 * t
                            last = pe.matmul(bank[3][:, at:at + 2], sq[:, t * P:(t + 1) * P], cst[:, C_HEAD:C_HEAD + 2],
                                             start=True, stop=True)
                    last.then_inc(ms_mm, 1)

                    def spread():
                        pe.wait_ge(kw_done, p + 1)
                        for t in range(TT):
                            last = pe.matmul(bank[3][:, t * P:(t + 1) * P], kwide[:, t, :], ident, start=True, stop=True)
                        last.then_inc(kb_mm, 1)

                    unit(ph, p, 2, hook=spread)
                if attends:
                    turn(2)
                    values(1)
                    turn(3)
                    values(2)
                if projects:
                    pe.wait_ge(evac, ph.group(p, 2) + 1 + EVAC_CREDIT)
                    pe.wait_ge(kn_done, p + 1)
                    for t in range(TT):
                        last = pe.transpose(bank[3][:, t * P:(t + 1) * P], vt[:, t * P:(t + 1) * P], ident)
                    last.then_inc(v_mm, 1)
                if attends:
                    values(3)

            for ph in phases:
                name = ph.name
                if name == "qkv":
                    attention(0, True, False, False)
                    with pe.Fori(1, PAIRS) as p:
                        attention(p, True, True, False)
                    attention(PAIRS, False, True, False)
                    continue

                def y_hook(i, j, name=name):
                    if name == "down3" and j == 2:
                        return lambda: turn_y(2 * i, 0)
                    if name == "down3" and j == 0 and not (isinstance(i, int) and i == 0):
                        return lambda: turn_y(2 * i - 1, 1)
                    return None

                def first(ph=ph, name=name):
                    if name in NORM_OF:
                        norm = NORM_OF[name]
                        unit(ph, 0, 0, waits=[(xl_done, chunk_base(norm) + k + 1) for k in range(KD)])
                        norm_mean(norm)
                        unit(ph, 0, 1, hook=lambda: norm_spread(norm))
                        rest = range(2, ph.per)
                    elif name.startswith("down"):
                        done = KF * ffn_of[name]
                        unit(ph, 0, 0, waits=[(hl_done, done + KF - 2)] + [None] * (KF // 2 - 1))
                        unit(ph, 0, 1, waits=[None] * (KF // 2 - 2) + [(hl_done, done + KF - 1), (hl_done, done + KF)])
                        rest = range(2, ph.per)
                    else:
                        of = al_done if name == "w_out" else ol_done
                        extra = 0 if name == "w_out" else OUT_CREDIT
                        unit(ph, 0, 0, waits=[(of, k + 1 + extra) for k in range(KD)])
                        rest = range(1, ph.per)
                    for j in rest:
                        unit(ph, 0, j, hook=y_hook(0, j))
                    if name == "w_in":
                        turn_u(0)
                        pe.wait_ge(mix_in, 16 * 7)
                        for n in range(4):
                            t, half = n // 2, n % 2
                            pe.matmul(bank[3 + n][:, :], h3[:, t * P:(t + 1) * P], fwo[:, half * HW:(half + 1) * HW],
                                      start=True, stop=True).then_inc(filt_mm, 1)

                def body(i, last, ph=ph, name=name):
                    for j in range(ph.per):
                        unit(ph, i, j, hook=y_hook(i, j))
                    if name == "w_in":
                        turn_u(i)

                first()
                with pe.Fori(1, ph.iters) as i:
                    body(i, False)
                if name == "down3":
                    turn_y(KD - 1, 1)
                if name == "w_in":
                    pe.wait_ge(filt_done, 8)
                    for n in range(4):
                        cs, m = n // 2, n % 2
                        for t in range(2):
                            last = pe.matmul(bank[3 + n][:, :], dft[:, cs, t, m * P:(m + 1) * P],
                                             (hdif if cs else hsum)[:, t, :], start=(t == 0), stop=(t == 1))
                        last.then_inc(kf_mm, 1)
                    pe.wait_ge(ut_done, KH)
                    pe.wait_ge(kf_done, 4)
                    for n in range(4):
                        s, m = n // 2, n % 2
                        if n >= 2:
                            pe.wait_ge(prod_done, 4 * (n - 1))
                        for cs in range(2):
                            for t in range(2):
                                last = pe.matmul(bank[3 + 2 * (n % 2) + cs][:, :], dft[:, cs, t, m * P:(m + 1) * P],
                                                 ut[:, 2 * s + t, :], start=(t == 0), stop=(t == 1))
                            last.then_inc(u_mm, 1)
                    for g in range(4):
                        pe.wait_ge(pooled, g + 1)
                        if g >= 2:
                            pe.wait_ge(al_done, g - 1)
                        pe.matmul(bank[7 if g % 2 else 2][:, :].rearrange("p (s t) -> p s t", s=NSEQ), poolw[:, g, :],
                                  ppad[:, g, :, PAD:PAD + SEQ], start=True, stop=True).then_inc(mix_mm, 1)
                    pe.wait_ge(prod_done, 16)
                    for c in range(KH):
                        for s in range(NSEQ):
                            if c == 0:
                                pe.wait_ge(spec_done, 4 * (s + 1))
                            for k in range(4):
                                last = pe.matmul(bank[3 + c][:, s * SEQ:(s + 1) * SEQ],
                                                 spec[:, s, k // 2, k % 2, c * P:(c + 1) * P], idft[:, k, :],
                                                 start=(k == 0), stop=(k == 3))
                        last.then_inc(inv_mm, 1)

        @block.gpsimd
        def _(pool):
            ph = by["w_in"]
            pool.wait_ge(unit_done, ph.unit0 + UNIT_CREDIT)
            pool.memset(ppad[:, :, :, :], 0.0).then_inc(pad_done, 1)
            pool.wait_ge(mix_in, 16 * 7)
            step = 0
            for g, w in enumerate(WINDOWS):
                if g:
                    pool.wait_ge(pooled, g)
                pool.wait_ge(evac, ph.group(g, 3) + 1 + EVAC_CREDIT)
                src, lo, hi = ppad[:, g, :, :], 0, PROW
                for n in range(g + 1):
                    back, ahead_ = (1, 0) if n == 0 else (2 ** (n - 1), 2 ** (n - 1))
                    lo, hi = lo + back, hi - ahead_
                    dst = win[n % 2]
                    pool.tensor_tensor(dst[:, :, lo:hi], src[:, :, lo - back:hi - back], src[:, :, lo + ahead_:hi + ahead_],
                                       ALU.add).then_inc(win_step, 1)
                    step += 1
                    pool.wait_ge(win_step, step)
                    src = dst
                mid = src[:, :, PAD:PAD + SEQ]
                inside = ppad[:, g, :, PAD:PAD + SEQ]
                pool.tensor_tensor(mid, mid, icnt[:, g:g + 1, :].to_broadcast([P, NSEQ, SEQ]), ALU.mult)\
                    .then_inc(win_step, 1)
                step += 1
                pool.wait_ge(win_step, step)
                pool.tensor_tensor(inside, mid, inside, ALU.subtract).then_inc(pooled, 1)
            for n in range(4):
                s, m = n // 2, n % 2
                part = [ga[0], ua[0]] if n % 2 == 0 else [ga[1], ua[1]]
                pool.wait_ge(prod_done, 4 * (n + 1))
                pool.tensor_tensor(spec[:, s, 0, m, :], spec[:, s, 0, m, :], part[0][:, :], ALU.subtract)\
                    .then_inc(spec_done, 1)
                pool.tensor_tensor(spec[:, s, 1, m, :], spec[:, s, 1, m, :], part[1][:, :], ALU.add)\
                    .then_inc(spec_done, 1)

            def mask(p, attends):
                pool.wait_ge(braw_in, 32 * (p + 1))
                if attends:
                    pool.wait_ge(mx_done, 4 * p)
                pool.tensor_tensor(bmask[:, :, :].rearrange("p h (r c) -> p (h r) c", c=GRID_W),
                                   braw[:, :, :].rearrange("p h (r c) -> p (h r) c", c=GRID_W),
                                   cst[:, C_MASK:C_MASK + GRID_W].unsqueeze(1).to_broadcast([P, 12, GRID_W]), ALU.add)\
                    .then_inc(mask_done, 1)

            mask(0, False)
            with pool.Fori(1, PAIRS) as p:
                mask(p, True)


def constants():
    small = np.zeros((P, C_ALL), np.float32)
    small[:, C_ID:C_ID + P] = np.eye(P)
    for h in range(2):
        small[h * HD:(h + 1) * HD, C_HEAD + h] = 1.0 / HD
    small[:, C_MEAN] = 1.0 / D
    small[:, C_EPS] = EPS
    t_norm = np.linspace(0.0, 1.0, SEQ, dtype=np.float32)
    small[:, C_T:C_T + 2] = -t_norm.reshape(2, P).T
    q = np.arange(P)[:, None] % GRID_W
    k = np.arange(GRID_W)[None, :]
    start = np.clip(q - NA_COLS // 2, 0, GRID_W - NA_COLS)
    small[:, C_MASK:C_MASK + GRID_W] = np.where((k >= start) & (k < start + NA_COLS), 0.0, -1e30)
    t, m = np.arange(SEQ), np.arange(NFREQ)
    angle = 2.0 * np.pi * (((2 * m[:, None] + 1) * t[None, :]) % (4 * SEQ)) / (4 * SEQ)
    trig = np.stack([np.cos(angle), np.sin(angle)])
    dft = np.zeros((P, 3, 2, 2, SEQ), np.float32)
    dft[:, 0] = trig.transpose(0, 2, 1).reshape(2, 2, P, NFREQ).transpose(2, 0, 1, 3)
    dft[:, 1] = (trig / NFREQ).reshape(2, 2, P, SEQ).transpose(2, 0, 1, 3)
    for g, w in enumerate(WINDOWS):
        lo, hi = np.clip(t - w // 2, 0, SEQ - 1), np.clip(t + w - w // 2 - 1, 0, SEQ - 1)
        dft[:, 2, g // 2, g % 2] = 1.0 / (hi - lo + 1)
    bands = np.linspace(1e-4, 15, 16, dtype=np.float32)
    angles = (np.float32(2.0 * np.pi / SEQ) * np.arange(SEQ, dtype=np.float32)[:, None]) * bands[None, :]
    z = np.concatenate([t_norm[:, None], np.cos(angles), -np.sin(angles)], axis=-1)
    return {"c_small": small, "c_dft": dft, "c_z": np.ascontiguousarray(z.T.astype(np.float32))}


_INS = ["x_prompt", "x_sample", "norm_g", "ffn_w_gate", "ffn_w_up", "ffn_w_down", "w_in_ab", "pool_w", "pool_scale",
        "short_w", "short_b", "filt_w1", "filt_b1", "filt_w2", "filt_b2", "filt_w3", "filt_b3", "filt_freq",
        "filt_w_out", "filt_deltas", "hyena_bias", "w_out_ab", "w_qkv", "q_norm_g", "k_norm_g", "rpb", "w_o"]


def kernel(**inputs):
    import concourse.bacc as bacc
    from concourse.bass_utils import run_bass_kernel_spmd

    nc = bacc.Bacc("TRN2", target_bir_lowering=False, num_devices=1)
    given = {name: np.ascontiguousarray(inputs[name]) for name in _INS}
    given.update(constants())
    arrays = {f"in_{name}": v for name, v in given.items()}
    args = {name: nc.dram_tensor(f"in_{name}", v.shape, mybir.dt.from_np(v.dtype), kind="ExternalInput").ap()
            for name, v in given.items()}
    outs = [nc.dram_tensor(name, (1, SEQ, D), F32, kind="ExternalOutput").ap() for name in ("y_prompt", "y_sample")]
    build_trunk(nc, args, *outs)
    got = run_bass_kernel_spmd(nc, [arrays], core_ids=[0]).results[0]
    return got["y_prompt"], got["y_sample"]
```

```python
from contextlib import ExitStack

import numpy as np

import concourse.bass as bass
from concourse import mybir

F32 = mybir.dt.float32
F32R = mybir.dt.float32r
ACT = mybir.ActivationFunctionType
ALU = mybir.AluOpType
AX = mybir.AxisListType

P = 128
D = 1024
KD = D // P
FF = 2816
KF = FF // P
SEQ = 256
NSEQ = 2
TOK = NSEQ * SEQ
TT = TOK // P
EPS = 1e-6
HEADS = 16
HD = 64
PAIRS = HEADS // 2
GRID_W = 64
ROWS = SEQ // GRID_W
RPB_R, RPB_C = 15, 31
DR = 2 * ROWS - 1
NA_COLS = 16
WINDOWS = (2, 4, 8, 16)
HW = 512
KH = HW // P
EMB, HID = 33, 64
NFREQ = SEQ
PAD = 8
PROW = SEQ + 2 * PAD
MAGIC = 1.5 * 2.0 ** 23
TWO_PI = 2.0 * np.pi
PI_A = 6.28125
PI_B = float(np.float32(np.round((TWO_PI - PI_A) * 2.0 ** 21) / 2.0 ** 21))
PI_C = float(np.float32(TWO_PI - PI_A - PI_B))
SIN_MAX = 3.1415925

C_ID, C_HEAD, C_MEAN, C_EPS, C_T, C_MASK, C_ALL = 0, 128, 130, 131, 132, 134, 198
V_NORM, V_PSCALE, V_SW, V_SB, V_GQ, V_GK, V_B1, V_FREQ, V_ALL = 0, 48, 52, 88, 100, 101, 102, 105, 106
UNIT_CREDIT, EVAC_CREDIT, LOW_CREDIT = 2, 2, 3
SCORE_CREDIT, TURN_CREDIT, VALUE_CREDIT, OUT_CREDIT, COPY_CREDIT, STORE_CREDIT = 4, 2, 2, 1, 1, 16


class Phase:

    def __init__(self, name, iters, slots, ktiles, groups_at):
        self.name, self.iters, self.slots, self.kt, self.groups_at = name, iters, slots, ktiles, groups_at
        self.per = slots
        self.gper = len(groups_at)

    def unit(self, i, j):
        return self.unit0 + self.per * i + j

    def group(self, i, j):
        return self.group0 + self.gper * i + self.groups_at.index(j)


def plan():
    up = lambda n: Phase(f"up{n}", KF // 2, 4, KD, [0, 1, 2, 3])
    down = lambda n: Phase(f"down{n}", KD // 2, 4, KF // 2, [1, 3])
    phases = [up(0), down(0), Phase("w_in", KH, 4, KD, [0, 1, 2, 3]), Phase("w_out", 2, 4, KD, [0, 1, 2, 3]),
              up(1), down(1), up(2), down(2), Phase("qkv", PAIRS, 3, KD, [0, 1, 2]),
              Phase("w_o", 2, 4, KD, [0, 1, 2, 3]), up(3), down(3)]
    unit, group, uses = 0, KD, [0] * 4
    for n, ph in enumerate(phases):
        ph.unit0, ph.group0, ph.uses0 = unit, group, list(uses)
        unit += ph.iters * ph.per
        group += ph.iters * ph.gper
        for s in range(ph.slots):
            uses[s] += ph.iters
        ph.next = phases[n + 1] if n + 1 < len(phases) else None
    return phases


def build_trunk(nc, a, y_prompt, y_sample):
    phases = plan()
    by = {ph.name: ph for ph in phases}
    NEXT_NORM = {"down0": 1, "w_out": 2, "down1": 3, "down2": 4, "w_o": 5}
    NEXT_NORM["down1"] = 3
    NORM_OF = {"up0": 0, "w_in": 1, "up1": 2, "up2": 3, "qkv": 4, "up3": 5}
    ffn_of = {"up0": 0, "down0": 0, "up1": 1, "down1": 1, "up2": 2, "down2": 2, "up3": 3, "down3": 3}

    wg = a["ffn_w_gate"].rearrange("l j (k p) f -> (l j) p k f", p=P)
    wu = a["ffn_w_up"].rearrange("l j (k p) f -> (l j) p k f", p=P)
    wd = a["ffn_w_down"].rearrange("l j (k p) d -> (l j) p k d", p=P)
    w_in = a["w_in_ab"].rearrange("o (k p) f -> (o p) k f", p=P)
    w_out = a["w_out_ab"].rearrange("o (k p) f -> (o p) k f", p=P)
    w_qkv = a["w_qkv"].rearrange("o (k p) f -> (o p) k f", p=P)
    w_o = a["w_o"].rearrange("o (k p) f -> (o p) k f", p=P)
    bias_dram = nc.dram_tensor("bias_by_column", [GRID_W, HEADS, DR * GRID_W], F32).ap()

    with ExitStack() as ctx:
        def sb(name, shape, dt=F32, where=ctx):
            return where.enter_context(nc.sbuf_tensor(name, shape, dt))

        def sem(name):
            return ctx.enter_context(nc.semaphore(name))

        x = sb("x", [P, KD, TOK])
        xh = sb("xh", [P, KD, TOK], F32R)
        xl = sb("xl", [P, KD, TOK], F32R)
        raw = [sb(f"raw{s}", [P, KF // 2, P]) for s in range(4)]
        wh = [sb(f"wh{s}", [P, KF // 2, P], F32R) for s in range(2)]
        wl = [sb(f"wl{s}", [P, KF // 2, P], F32R) for s in range(2)]
        rbc = sb("rbc", [P, TOK])
        sqacc = sb("sqacc", [P, TOK])
        sqtmp = sb("sqtmp", [P, 2, TOK])
        ga = [sb(f"ga{s}", [P, TOK]) for s in range(2)]
        ua = [sb(f"ua{s}", [P, TOK]) for s in range(2)]
        rwide = sb("rwide", [P, TT, P])
        rcol = sb("rcol", [P, TT])
        cst = sb("cst", [P, C_ALL])
        vrow = sb("vrow", [V_ALL, P])
        vec = sb("vec", [P, V_ALL])
        gqk = sb("gqk", [P, 1])
        zT, fw1, fw2, fw3 = sb("zT", [EMB, SEQ]), sb("fw1", [EMB, HID]), sb("fw2", [HID, HID]), sb("fw3", [HID, HID])
        h3 = sb("h3", [HID, SEQ])
        fa, fk, fh = ga[0][0:HID, 0:SEQ], ga[1][0:HID, 0:SEQ], ua[0][0:HID, 0:SEQ]
        ident = cst[:, C_ID:C_ID + P]

        def region(rows):
            own = ExitStack()
            got = [sb(*r, where=own) for r in rows]
            own.close()
            return got

        hh, hl = region([("hh", [P, KF, TOK], F32R), ("hl", [P, KF, TOK], F32R)])
        (xrow,) = region([("xrow", [P, TT, D])])
        own = ExitStack()
        dft = sb("dft", [P, 2, 2, NFREQ], where=own)
        idft = sb("idft", [P, 4, SEQ], where=own)
        icnt = sb("icnt", [P, 4, SEQ], where=own)
        kf = sb("kf", [P, 2, 2, HW], where=own)
        x0 = sb("x0", [P, KH, TOK], where=own)
        ppad = sb("ppad", [P, 4, NSEQ, PROW], where=own)
        win = [sb(f"win{s}", [P, NSEQ, PROW], where=own) for s in range(2)]
        up = sb("up", [P, TOK], where=own)
        poolw = sb("poolw", [P, 4, P], where=own)
        inner = ExitStack()
        decay, filt = sb("decay", [P, 2, 2, HW], where=inner), sb("filt", [P, 2, 2, HW], where=inner)
        inner.close()
        spec = sb("spec", [P, NSEQ, 2, 2, HW], where=own)
        inner = ExitStack()
        absd, hsum = sb("absd", [P, 2 * HW], where=inner), sb("hsum", [P, 2, HW], where=inner)
        hdif, ut = sb("hdif", [P, 2, HW], where=inner), sb("ut", [P, TT, HW], where=inner)
        hbias, fwo = sb("hbias", [1, HW], where=inner), sb("fwo", [HID, 2 * HW], where=inner)
        inner.close()
        ah, al = sb("ah", [P, KD, TOK], F32R, where=own), sb("al", [P, KD, TOK], F32R, where=own)
        own.close()
        (wh2, wl2, qt, kt, vt, sqq, sqk, qs, kn, vs, braw, bmask, sc, pt, oh, ol, rsum, nmax, rqk, kwide) = region([
            ("wh2", [P, KD, P], F32R), ("wl2", [P, KD, P], F32R), ("qt", [P, TOK]), ("kt", [P, TOK]), ("vt", [P, TOK]),
            ("sqq", [P, TOK]), ("sqk", [P, TOK]), ("qs", [P, TOK]), ("kn", [P, TOK]), ("vs", [P, TT, P]),
            ("braw", [P, 2, 6 * GRID_W]), ("bmask", [P, 2, 6 * GRID_W]), ("sc", [P, 2, 2, SEQ]), ("pt", [P, 2, 2, SEQ]),
            ("oh", [P, KD, TOK], F32R), ("ol", [P, KD, TOK], F32R), ("rsum", [P, 2, 2]), ("nmax", [P, 2, 2]),
            ("rqk", [P, 2, TT, 2]), ("kwide", [P, TT, P])])
        wh, wl = wh + [wh2], wl + [wl2]

        bank = [ctx.enter_context(nc.psum_tensor(f"bank{b}", [P, TOK], F32)) for b in range(8)]

        raw_in = [sem(f"raw_in{s}") for s in range(4)]
        const_in, vec_in, filt_in, out_in = sem("const_in"), sem("vec_in"), sem("filt_in"), sem("out_in")
        x_in = [sem(f"x_in{s}") for s in range(TT)]
        mix_in, toep_in, braw_in = sem("mix_in"), sem("toep_in"), sem("braw_in")
        high, low, unit_done, evac = sem("high"), sem("low"), sem("unit_done"), sem("evac")
        xh_done, xl_done, sq_done, acc_done = sem("xh_done"), sem("xl_done"), sem("sq_done"), sem("acc_done")
        mean_mm, std_done, rwide_done, rbc_mm, rbc_done = (sem("mean_mm"), sem("std_done"), sem("rwide_done"),
                                                           sem("rbc_mm"), sem("rbc_done"))
        silu_done, h_done, hh_done, hl_done = sem("silu_done"), sem("h_done"), sem("hh_done"), sem("hl_done")
        vec_mm, vec_done, f_mm, f_step, f_sin = sem("vec_mm"), sem("vec_done"), sem("f_mm"), sem("f_step"), sem("f_sin")
        f_clamp, x_mm, pv_mm = sem("f_clamp"), sem("x_mm"), sem("pv_mm")
        dec_done, filt_mm, filt_done = sem("dec_done"), sem("filt_mm"), sem("filt_done")
        conv_done, tap_done, u_done, ut_mm, ut_done = (sem("conv_done"), sem("tap_done"), sem("u_done"), sem("ut_mm"),
                                                       sem("ut_done"))
        pad_done, win_step, pooled = sem("pad_done"), sem("win_step"), sem("pooled")
        kf_mm, kf_done, u_mm, prod_done, spec_done = (sem("kf_mm"), sem("kf_done"), sem("u_mm"), sem("prod_done"),
                                                      sem("spec_done"))
        mix_mm, inv_mm, gated, ah_done, al_done = (sem("mix_mm"), sem("inv_mm"), sem("gated"), sem("ah_done"),
                                                   sem("al_done"))
        s_mm, s_used, mx_done, exp_done, rs_done, p_done = (sem("s_mm"), sem("s_used"), sem("mx_done"), sem("exp_done"),
                                                            sem("rs_done"), sem("p_done"))
        t_mm, t_done, oh_done, ol_done = sem("t_mm"), sem("t_done"), sem("oh_done"), sem("ol_done")
        sqq_done, sqk_done, ms_mm, ms_std, kw_done = (sem("sqq_done"), sem("sqk_done"), sem("ms_mm"), sem("ms_std"),
                                                      sem("kw_done"))
        rqk_done = sem("rqk_done")
        kb_mm, kn_done, qs_done, v_mm, vs_done = (sem("kb_mm"), sem("kn_done"), sem("qs_done"), sem("v_mm"),
                                                  sem("vs_done"))
        mask_done, gqk_done, y_ready, y_mm, y_copied = (sem("mask_done"), sem("gqk_done"), sem("y_ready"), sem("y_mm"),
                                                        sem("y_copied"))
        y_out = [sem(f"y_out{s}") for s in range(2)]

        block = ctx.enter_context(nc.Block())

        def settle(eng):
            eng.wait_ge(low, LOW_CREDIT)

        def unit_bank(ph, j):
            if ph.name == "qkv":
                return (0, 1, 0)[j]
            return j // 2 if ph.name.startswith("down") else j

        def unit_source(ph, i, j):
            if ph.name.startswith("up"):
                return (wu if j % 2 else wg)[ffn_of[ph.name], :, :, bass.ds((2 * i + j // 2) * P, P)]
            if ph.name.startswith("down"):
                return wd[ffn_of[ph.name], :, (j % 2) * (KF // 2):(j % 2 + 1) * (KF // 2),
                          bass.ds((2 * i + j // 2) * P, P)]
            if ph.name == "w_in":
                return w_in[:, :, bass.ds((3 - j) * HW + i * P, P)]
            if ph.name == "qkv":
                return w_qkv[:, :, bass.ds(j * D + i * P, P)]
            return (w_out if ph.name == "w_out" else w_o)[:, :, bass.ds((4 * i + j) * P, P)]

        @block.sync
        def _(sp):
            for n in range(4):
                half = slice(n // 2 * (D // 2), (n // 2 + 1) * (D // 2))
                sp.dma_start(xrow[:, n % 2 * 2:n % 2 * 2 + 2, half],
                             (a["x_sample"] if n % 2 else a["x_prompt"])[0].rearrange("(t p) c -> p t c", p=P)[:, :, half])\
                  .then_inc(x_in[n], 16)

            def load(ph, i):
                for j in range(ph.per):
                    sp.wait_ge(low, ph.unit(i, j) - 2 + LOW_CREDIT)
                    sp.dma_start(raw[j][:, 0:ph.kt, :], unit_source(ph, i, j)).then_inc(raw_in[j], 16)

            for ph in phases:
                if ph.name == "w_in":
                    for i in range(ph.iters):
                        load(ph, i)
                else:
                    with sp.Fori(0, ph.iters) as i:
                        load(ph, i)

        def split_place(ph, j):
            return (j if ph.name == "qkv" else j % 2), j

        def ahead(ph, i, j, last):
            if j + 2 < ph.per:
                return ph, i, j + 2
            if last:
                return (ph.next, 0, j + 2 - ph.per) if ph.next else (None, 0, 0)
            return ph, i + 1, j + 2 - ph.per

        def split_high(act, ph, i, j):
            if ph is None:
                return
            w, r = split_place(ph, j)
            act.wait_ge(raw_in[r], 16 * (ph.uses0[r] + 1 + i))
            act.wait_ge(unit_done, ph.unit(i, j) - 1 + UNIT_CREDIT)
            act.activation(wh[w][:, 0:ph.kt, :], raw[r][:, 0:ph.kt, :], ACT.Copy).then_inc(high, 1)

        def split_low(dve, ph, i, j):
            if ph is None:
                return
            w, r = split_place(ph, j)
            dve.wait_ge(high, ph.unit(i, j) + 1)
            dve.tensor_tensor(wl[w][:, 0:ph.kt, :], raw[r][:, 0:ph.kt, :], wh[w][:, 0:ph.kt, :].bitcast(F32),
                              ALU.subtract).then_inc(low, 1)

        def chunk_base(norm):
            return KD * norm

        def out_chunk(ph, i, j):
            return 2 * i + j // 2 if ph.name.startswith("down") else 4 * i + j

        def phase_loop(eng, ph, body, after_first=None, first=0):
            if after_first:
                body(0, False)
                after_first()
                first = 1
            if ph.iters - 1 > first:
                with eng.Fori(first, ph.iters - 1) as i:
                    body(i, False)
            body(ph.iters - 1, True)

        @block.scalar
        def _(act):
            col = lambda n: vec[:, bass.ds(n, 1)]

            act.dma_start(cst[:, :], a["c_small"]).then_inc(const_in, 16)
            act.dma_start(vrow[:, :], a["v_params"]).then_inc(vec_in, 16)
            act.dma_start(zT[:, :], a["c_z"]).then_inc(filt_in, 16)
            act.dma_start(fw1[:, :], a["filt_w1"][0]).then_inc(filt_in, 16)
            act.dma_start(fw2[:, :], a["filt_w2"][0]).then_inc(filt_in, 16)
            act.dma_start(fw3[:, :], a["filt_w3"][0]).then_inc(filt_in, 16)

            def residual(ph, i, j, norm):
                d = out_chunk(ph, i, j)
                act.wait_ge(evac, ph.group(i, j) + 1 + EVAC_CREDIT)
                settle(act)
                residual_parts(norm, d, j // 2 % 2 if ph.name.startswith("down") else j % 2)

            def residual_parts(norm, d, parity):
                act.activation(xh[:, bass.ds(d, 1), :], x[:, bass.ds(d, 1), :], ACT.Copy,
                               scale=col(V_NORM + norm * KD + d)).then_inc(xh_done, 1)
                act.activation(sqtmp[:, parity, :], x[:, bass.ds(d, 1), :], ACT.Square).then_inc(sq_done, 1)

            def norm_std(norm):
                act.wait_ge(mean_mm, norm + 1)
                act.activation(rcol[:, :], bank[7][:, 0:TT], ACT.Sqrt, bias=cst[:, C_EPS:C_EPS + 1]).then_inc(std_done, 1)

            def evacuate(ph, i, j):
                if ph.name.startswith("up"):
                    f = 2 * i + j // 2
                    g, u = ga[j // 2], ua[j // 2]
                    if j % 2 == 0:
                        act.wait_ge(evac, ph.group(i, j) + 1 + EVAC_CREDIT)
                        act.activation(g[:, :], g[:, :], ACT.Silu).then_inc(silu_done, 1)
                    else:
                        act.wait_ge(h_done, KF * ffn_of[ph.name] + f + 1)
                        settle(act)
                        act.activation(hh[:, bass.ds(f, 1), :], u[:, :], ACT.Copy).then_inc(hh_done, 1)
                elif ph.name in NEXT_NORM:
                    if j in ph.groups_at:
                        residual(ph, i, j, NEXT_NORM[ph.name])
                elif ph.name == "down3":
                    if j in ph.groups_at:
                        s, d = j // 2, out_chunk(ph, i, j)
                        act.wait_ge(y_mm, d + 1)
                        act.wait_ge(y_out[s], 32 * i + STORE_CREDIT)
                        act.activation(ua[s][:, :], bank[2 + s][:, :], ACT.Copy).then_inc(y_copied, 1)
                        act.wait_ge(y_copied, d + 1 + COPY_CREDIT)
                        for n, y in enumerate((y_prompt, y_sample)):
                            act.dma_start(y[0].rearrange("(t p) c -> p t c", p=P)[:, :, bass.ds(d * P, P)],
                                          ua[s][:, n * SEQ:(n + 1) * SEQ].rearrange("p (t c) -> p t c", t=2))\
                               .then_inc(y_out[s], 16)
                elif ph.name == "w_in":
                    if j < 3:
                        at = (2 - j) * KH + i
                        dst = x0[:, bass.ds(i, 1), :] if j == 2 else ua[j][:, :]
                        act.wait_ge(evac, ph.group(i, j) + 1 + EVAC_CREDIT)
                        settle(act)
                        act.activation(dst, ga[j % 2][:, :], ACT.Identity, bias=col(V_SB + at),
                                       scale=col(V_SW + 3 * KH + at)).then_inc(conv_done, 1)
                    else:
                        act.wait_ge(ut_mm, i + 1)
                        settle(act)
                        act.activation(ut[:, :, bass.ds(i * P, P)], bank[7][:, :].rearrange("p (t c) -> p t c", t=TT),
                                       ACT.Copy).then_inc(ut_done, 1)

            for d in range(KD):
                act.wait_ge(evac, d + 1 + EVAC_CREDIT)
                if d >= 2:
                    act.wait_ge(acc_done, d - 1)
                residual_parts(0, d, d % 2)
                if d == 1:
                    split_high(act, phases[0], 0, 0)
            split_high(act, phases[0], 0, 1)
            for r in range(DR):
                src = bass.AP(a["rpb"].tensor, (RPB_R // 2 - ROWS + 1 + r) * RPB_C + RPB_C // 2,
                              [[RPB_R * RPB_C, HEADS], [-1, GRID_W], [1, GRID_W]])
                act.dma_start(bias_dram[:, :, r * GRID_W:(r + 1) * GRID_W].rearrange("q h c -> h q c"), src)\
                   .then_inc(toep_in, 16)

            def attention(p, projects, attends, last):
                ph = by["qkv"]
                if projects:
                    if attends:
                        act.wait_ge(mask_done, p)
                    else:
                        act.wait_ge(toep_in, 16 * DR)
                    for half in range(2):
                        act.dma_start(braw[half * HD:(half + 1) * HD, :, :],
                                      bias_dram[:, bass.ds(2 * p, 2), (1 - half) * GRID_W:(7 - half) * GRID_W])\
                           .then_inc(braw_in, 16)
                    split_high(act, *ahead(ph, p, 0, last))
                    act.wait_ge(evac, ph.group(p, 0) + 1 + EVAC_CREDIT)
                    act.activation(sqq[:, :], qt[:, :], ACT.Square).then_inc(sqq_done, 1)

                def exps(h):
                    n = 4 * (p - 1) + h
                    act.wait_ge(mx_done, n + 1)
                    for t in range(2):
                        act.activation(sc[:, h % 2, t, :], sc[:, h % 2, t, :], ACT.Exp, bias=nmax[:, h % 2, t:t + 1],
                                       accum_out=rsum[:, h % 2, t:t + 1]).then_inc(exp_done, 1)

                def probs_t(h):
                    n = 4 * (p - 1) + h
                    act.wait_ge(t_mm, n + 1)
                    act.wait_ge(pv_mm, n - 1 + VALUE_CREDIT)
                    act.activation(pt[:, h % 2, :, :], bank[2 if h % 2 else 6][:, :].rearrange("p (k q) -> p k q", k=2), ACT.Copy)\
                       .then_inc(t_done, 1)

                if attends:
                    exps(0)
                    exps(1)
                if projects:
                    split_high(act, *ahead(ph, p, 1, last))
                    act.wait_ge(evac, ph.group(p, 1) + 1 + EVAC_CREDIT)
                    act.activation(sqk[:, :], kt[:, :], ACT.Square).then_inc(sqk_done, 1)
                if attends:
                    probs_t(0)
                    probs_t(1)
                    exps(2)
                    exps(3)
                if projects:
                    act.wait_ge(ms_mm, p + 1)
                    act.activation(rqk[:, :, :, :], bank[3][:, 0:4 * TT].rearrange("p (a t h) -> p a t h", a=2, t=TT),
                                   ACT.Sqrt, bias=cst[:, C_EPS:C_EPS + 1]).then_inc(ms_std, 1)
                    if attends:
                        act.wait_ge(s_mm, 4 * p)
                    act.activation(qs[:, :], qt[:, :], ACT.Copy, scale=gqk[:, 0:1]).then_inc(qs_done, 1)
                    split_high(act, *ahead(ph, p, 2, last))
                if attends:
                    probs_t(2)
                    probs_t(3)
                if projects:
                    act.wait_ge(v_mm, p + 1)
                    if attends:
                        act.wait_ge(pv_mm, 4 * p + VALUE_CREDIT)
                    act.activation(vs[:, :, :], bank[3][:, :].rearrange("p (t c) -> p t c", t=TT), ACT.Copy)\
                       .then_inc(vs_done, 1)
                if attends:
                    act.wait_ge(pv_mm, 4 * p + VALUE_CREDIT)
                    settle(act)
                    act.activation(oh[:, bass.ds(p - 1, 1), :], bank[7][:, :], ACT.Copy).then_inc(oh_done, 1)

            def main_body(ph):
                def body(i, last):
                    for j in range(ph.per):
                        if last and ph.next:
                            evacuate(ph, i, j)
                        split_high(act, *ahead(ph, i, j, last))
                        if not last or not ph.next:
                            evacuate(ph, i, j)
                return body

            for ph in phases:
                if ph.name == "w_in":
                    act.wait_ge(unit_done, ph.unit0 + UNIT_CREDIT)
                    act.dma_start(absd[:, :], a["filt_deltas"].to_broadcast([P, 2 * HW])).then_inc(mix_in, 16)
                    act.dma_start(fwo[:, :], a["filt_w_out"][0]).then_inc(mix_in, 16)
                    act.dma_start(hbias[:, :], a["hyena_bias"]).then_inc(mix_in, 16)
                    act.dma_start(poolw[:, :, :], a["pool_w"][0].rearrange("g c d -> c g d")).then_inc(mix_in, 16)
                    act.dma_start(dft[:, :, :, :], a["c_dft"][:, 0]).then_inc(mix_in, 16)
                    act.dma_start(idft[:, :, :], a["c_dft"][:, 1].rearrange("p a b m -> p (a b) m")).then_inc(mix_in, 16)
                    act.dma_start(icnt[:, :, :], a["c_dft"][:, 2].rearrange("p a b m -> p (a b) m")).then_inc(mix_in, 16)
                if ph.name in NORM_OF:
                    norm_std(NORM_OF[ph.name])
                if ph.name == "down0":
                    for j in range(4):
                        split_high(act, *ahead(ph, 0, j, False))
                        evacuate(ph, 0, j)
                        if j < 3:
                            act.wait_ge(f_step, 6 * (j + 1))
                            act.activation((fh if j < 2 else h3)[:, :], fa[:, :], ACT.Sin).then_inc(f_sin, 1)
                    phase_loop(act, ph, main_body(ph), first=1)
                    continue
                if ph.name == "qkv":
                    attention(0, True, False, False)
                    with act.Fori(1, PAIRS - 1) as p:
                        attention(p, True, True, False)
                    attention(PAIRS - 1, True, True, True)
                    attention(PAIRS, False, True, False)
                    continue

                def decays():
                    act.wait_ge(mix_in, 16 * 7)
                    act.activation(absd[:, :], absd[:, :], ACT.Abs).then_inc(dec_done, 1)
                    act.wait_ge(dec_done, 1)
                    for t in range(2):
                        act.activation(decay[:, t, :, :].rearrange("p a c -> p (a c)"), absd[:, :], ACT.Exp,
                                       scale=cst[:, C_T + t:C_T + t + 1]).then_inc(dec_done, 1)

                phase_loop(act, ph, main_body(ph), after_first=decays if ph.name == "w_in" else None)
                if ph.name == "w_in":
                    for n in range(4):
                        act.wait_ge(kf_mm, n + 1)
                        act.activation(kf[:, n // 2, n % 2, :], bank[4 + n][:, :], ACT.Copy).then_inc(kf_done, 1)
                    for g in range(4):
                        act.wait_ge(mix_mm, g + 1)
                        act.activation(ah[:, g, :], bank[2 + g % 2][:, :], ACT.Copy,
                                       scale=col(V_PSCALE + g)).then_inc(ah_done, 1)
                    for c in range(KH):
                        act.wait_ge(gated, c + 1)
                        act.activation(ah[:, 4 + c, :], x0[:, c, :], ACT.Copy).then_inc(ah_done, 1)
            for s in range(2):
                act.wait_ge(y_out[s], 16 * KD + STORE_CREDIT)

        @block.vector
        def _(dve):
            col = lambda n, rows=P: vec[0:rows, bass.ds(n, 1)]

            dve.memset(sqacc[:, :], 0.0).then_inc(low, LOW_CREDIT)
            for n, (s, credit) in enumerate(((unit_done, UNIT_CREDIT), (evac, EVAC_CREDIT), (s_used, SCORE_CREDIT),
                                             (t_done, TURN_CREDIT), (pv_mm, VALUE_CREDIT), (ol_done, OUT_CREDIT),
                                             (y_copied, COPY_CREDIT), (y_out[0], STORE_CREDIT), (y_out[1], STORE_CREDIT))):
                dve.memset(sqtmp[:, 0, n:n + 1], 0.0).then_inc(s, credit)
            dve.wait_ge(low, LOW_CREDIT)
            dve.wait_ge(vec_mm, 1)
            dve.tensor_copy(vec[:, :], bank[7][:, 0:V_ALL]).then_inc(vec_done, 1)
            dve.wait_ge(vec_done, 1)
            dve.scalar_tensor_tensor(out=gqk[:, :], in0=vec[:, V_GQ:V_GQ + 1], scalar=HD ** -0.5,
                                     in1=vec[:, V_GK:V_GK + 1], op0=ALU.mult, op1=ALU.mult).then_inc(gqk_done, 1)

            def filter_layer(n):
                s = 6 * n
                dve.wait_ge(f_mm, n + 1)
                dve.tensor_scalar(fa[:, :], bank[6][0:HID, 0:SEQ], col(V_B1 + n, HID), col(V_FREQ, HID),
                                  ALU.add, ALU.mult).then_inc(f_step, 1)
                dve.wait_ge(f_step, s + 1)
                dve.tensor_scalar(fk[:, :], fa[:, :], 1.0 / TWO_PI, MAGIC, ALU.mult, ALU.add).then_inc(f_step, 1)
                dve.wait_ge(f_step, s + 2)
                dve.tensor_scalar(fk[:, :], fk[:, :], MAGIC, None, ALU.subtract).then_inc(f_step, 1)
                for m, part in enumerate((PI_A, PI_B, PI_C)):
                    dve.wait_ge(f_step, s + 3 + m)
                    ins = dve.scalar_tensor_tensor(out=fa[:, :], in0=fk[:, :], scalar=-part, in1=fa[:, :],
                                                   op0=ALU.mult, op1=ALU.add)
                    if m < 2:
                        ins.then_inc(f_step, 1)
                    else:
                        ins.then_inc(f_clamp, 1)
                dve.wait_ge(f_clamp, n + 1)
                dve.tensor_scalar(fa[:, :], fa[:, :], SIN_MAX, -SIN_MAX, ALU.min, ALU.max).then_inc(f_step, 1)

            def part_low(norm, d):
                dve.wait_ge(xh_done, chunk_base(norm) + d + 1)
                dve.scalar_tensor_tensor(out=xl[:, bass.ds(d, 1), :], in0=x[:, bass.ds(d, 1), :],
                                         scalar=col(V_NORM + norm * KD + d), in1=xh[:, bass.ds(d, 1), :].bitcast(F32),
                                         op0=ALU.mult, op1=ALU.subtract).then_inc(xl_done, 1)

            def residual_low(norm, d, parity):
                part_low(norm, d)
                dve.wait_ge(sq_done, chunk_base(norm) + d + 1)
                dve.wait_ge(acc_done, chunk_base(norm) + d)
                dve.tensor_tensor(sqacc[:, :], sqacc[:, :], sqtmp[:, parity, :], ALU.add).then_inc(acc_done, 1)

            def norm_factor(norm):
                dve.wait_ge(std_done, norm + 1)
                dve.reciprocal(rcol[:, :], rcol[:, :]).then_inc(rwide_done, 1)
                dve.wait_ge(rwide_done, 2 * norm + 1)
                dve.tensor_copy(rwide[:, :, :], rcol[:, :].unsqueeze(2).to_broadcast([P, TT, P])).then_inc(rwide_done, 1)
                dve.wait_ge(rbc_mm, norm + 1)
                dve.tensor_copy(rbc[:, :], bank[7][:, :]).then_inc(rbc_done, 1)
                dve.memset(sqacc[:, :], 0.0).then_inc(rbc_done, 1)
                dve.wait_ge(rbc_done, 2 * norm + 2)

            def scaled(ph, i, j, out, b, shape=None):
                dve.wait_ge(unit_done, ph.unit(i, j) + 1 + UNIT_CREDIT)
                src, r = bank[b][:, :], rbc[:, :]
                if shape:
                    src, r = src.rearrange(shape, s=NSEQ), r.rearrange(shape, s=NSEQ)
                dve.tensor_tensor(out, src, r, ALU.mult).then_inc(evac, 1)

            def evacuate(ph, i, j):
                if ph.name.startswith("up"):
                    n, f = KF * ffn_of[ph.name], 2 * i + j // 2
                    g, u = ga[j // 2], ua[j // 2]
                    scaled(ph, i, j, (u if j % 2 else g)[:, :], j)
                    if j % 2:
                        dve.wait_ge(silu_done, n + f + 1)
                        dve.wait_ge(evac, ph.group(i, j) + 1 + EVAC_CREDIT)
                        dve.tensor_tensor(u[:, :], g[:, :], u[:, :], ALU.mult).then_inc(h_done, 1)
                        dve.wait_ge(hh_done, n + f + 1)
                        dve.tensor_tensor(hl[:, bass.ds(f, 1), :], u[:, :], hh[:, bass.ds(f, 1), :].bitcast(F32),
                                          ALU.subtract).then_inc(hl_done, 1)
                elif ph.name == "w_in":
                    if j == 3:
                        scaled(ph, i, j, ppad[:, bass.ds(i, 1), :, PAD:PAD + SEQ].rearrange("p o s t -> p (o s) t"), 3,
                               "p (s t) -> p s t")
                        return
                    n = 3 * i + j
                    src = ga[j % 2]
                    if not isinstance(n, int) or n > 0:
                        dve.wait_ge(tap_done, 2 * n)
                    scaled(ph, i, j, src[:, :], j)
                    dst = x0[:, bass.ds(i, 1), :] if j == 2 else ua[j][:, :]
                    dst = dst.rearrange("p o (s t) -> p (o s) t", s=NSEQ) if j == 2 else dst.rearrange("p (s t) -> p s t", s=NSEQ)
                    src = src[:, :].rearrange("p (s t) -> p s t", s=NSEQ)
                    at = (2 - j) * KH + i
                    dve.wait_ge(conv_done, n + 1)
                    dve.scalar_tensor_tensor(out=dst[:, :, 1:SEQ], in0=src[:, :, 0:SEQ - 1], scalar=col(V_SW + at),
                                             in1=dst[:, :, 1:SEQ], op0=ALU.mult, op1=ALU.add).then_inc(tap_done, 1)
                    dve.wait_ge(tap_done, 2 * n + 1)
                    dve.scalar_tensor_tensor(out=dst[:, :, 0:SEQ - 1], in0=src[:, :, 1:SEQ],
                                             scalar=col(V_SW + 6 * KH + at), in1=dst[:, :, 0:SEQ - 1],
                                             op0=ALU.mult, op1=ALU.add).then_inc(tap_done, 1)
                    if j == 1:
                        dve.wait_ge(tap_done, 2 * n + 2)
                        dve.tensor_tensor(up[:, :], ua[0][:, :], ua[1][:, :], ALU.mult).then_inc(u_done, 1)
                elif j in ph.groups_at:
                    d = out_chunk(ph, i, j)
                    parity = j // 2 % 2 if ph.name.startswith("down") else j % 2
                    factor = 0.5 if ph.name.startswith("down") else 1.0
                    b = unit_bank(ph, j)
                    dve.wait_ge(unit_done, ph.unit(i, j) + 1 + UNIT_CREDIT)
                    out = ga[parity][:, :] if ph.name == "down3" else x[:, bass.ds(d, 1), :]
                    dve.scalar_tensor_tensor(out=out, in0=bank[b][:, :], scalar=factor, in1=x[:, bass.ds(d, 1), :],
                                             op0=ALU.mult, op1=ALU.add).then_inc(evac, 1)
                    if ph.name != "down3":
                        residual_low(NEXT_NORM[ph.name], d, parity)

            for d in range(KD):
                dve.wait_ge(x_mm, d + 1)
                dve.tensor_copy(x[:, d, :], bank[d][:, :]).then_inc(evac, 1)
            split_low(dve, phases[0], 0, 0)
            for d in range(KD):
                part_low(0, d)
            split_low(dve, phases[0], 0, 1)

            def attention(p, projects, attends, last):
                ph = by["qkv"]

                def maxima(h):
                    s, a_ = h // 2, h % 2
                    n = 4 * (p - 1) + h
                    dve.wait_ge(s_mm, n + 1)
                    for t in range(2):
                        dve.scalar_tensor_tensor(out=sc[:, h % 2, t, :], in0=bank[4 + h % 2][:, t * SEQ:(t + 1) * SEQ],
                                                 scalar=rqk[:, 0, 2 * s + t, a_:a_ + 1],
                                                 in1=bmask[:, a_, (2 - 2 * t) * GRID_W:(6 - 2 * t) * GRID_W],
                                                 op0=ALU.mult, op1=ALU.add).then_inc(s_used, 1)
                    dve.wait_ge(s_used, 2 * (n + 1) + SCORE_CREDIT)
                    dve.tensor_reduce(nmax[:, h % 2, :], sc[:, h % 2, :, :], AX.X, ALU.max, negate=True)\
                       .then_inc(mx_done, 1)

                def normalise(h):
                    n = 4 * (p - 1) + h
                    dve.wait_ge(exp_done, 2 * n + 2)
                    dve.reciprocal(rsum[:, h % 2, :], rsum[:, h % 2, :]).then_inc(rs_done, 1)
                    dve.wait_ge(rs_done, n + 1)
                    for t in range(2):
                        dve.tensor_scalar(sc[:, h % 2, t, :], sc[:, h % 2, t, :], rsum[:, h % 2, t:t + 1], None,
                                          ALU.mult).then_inc(p_done, 1)

                if projects:
                    if attends:
                        dve.wait_ge(qs_done, p)
                    scaled(ph, p, 0, qt[:, :], 0)
                    split_low(dve, *ahead(ph, p, 0, last))
                if attends:
                    dve.wait_ge(mask_done, p)
                    maxima(0)
                    maxima(1)
                    normalise(0)
                    normalise(1)
                if projects:
                    scaled(ph, p, 1, kt[:, :], 1)
                    split_low(dve, *ahead(ph, p, 1, last))
                if attends:
                    maxima(2)
                    maxima(3)
                    normalise(2)
                    normalise(3)
                if projects:
                    dve.wait_ge(ms_std, p + 1)
                    dve.reciprocal(rqk[:, :, :, :], rqk[:, :, :, :]).then_inc(rqk_done, 1)
                    dve.wait_ge(rqk_done, p + 1)
                    dve.tensor_copy(kwide[:, :, :].rearrange("p t (h c) -> p t h c", h=2),
                                    rqk[:, 1, :, :].unsqueeze(3).to_broadcast([P, TT, 2, HD])).then_inc(kw_done, 1)
                    dve.wait_ge(kb_mm, p + 1)
                    if attends:
                        dve.wait_ge(s_mm, 4 * p)
                    dve.tensor_tensor(kn[:, :], kt[:, :], bank[3][:, :], ALU.mult).then_inc(kn_done, 1)
                    if attends:
                        dve.wait_ge(v_mm, p)
                    scaled(ph, p, 2, vt[:, :], 0)
                    split_low(dve, *ahead(ph, p, 2, last))
                if attends:
                    dve.wait_ge(oh_done, p)
                    dve.tensor_tensor(ol[:, bass.ds(p - 1, 1), :], bank[7][:, :],
                                      oh[:, bass.ds(p - 1, 1), :].bitcast(F32), ALU.subtract).then_inc(ol_done, 1)

            def main_body(ph):
                def body(i, last):
                    for j in range(ph.per):
                        if last and ph.next:
                            evacuate(ph, i, j)
                        split_low(dve, *ahead(ph, i, j, last))
                        if not last or not ph.next:
                            evacuate(ph, i, j)
                return body

            for ph in phases:
                if ph.name == "w_in":
                    dve.wait_ge(pad_done, 1)
                if ph.name in NORM_OF:
                    norm_factor(NORM_OF[ph.name])
                if ph.name == "down0":
                    for j in range(4):
                        split_low(dve, *ahead(ph, 0, j, False))
                        evacuate(ph, 0, j)
                        if j < 3:
                            filter_layer(j)
                    phase_loop(dve, ph, main_body(ph), first=1)
                    continue
                if ph.name == "qkv":
                    attention(0, True, False, False)
                    with dve.Fori(1, PAIRS - 1) as p:
                        attention(p, True, True, False)
                    attention(PAIRS - 1, True, True, True)
                    attention(PAIRS, False, True, False)
                    continue

                def filter_in_time():
                    for t in range(2):
                        for half in range(2):
                            n = 2 * t + half
                            dve.wait_ge(filt_mm, n + 1)
                            dve.wait_ge(dec_done, 2 + t)
                            dve.scalar_tensor_tensor(out=filt[:, t, half, :], in0=decay[:, t, half, :], scalar=0.05,
                                                     in1=bank[4 + n][:, :], op0=ALU.add, op1=ALU.mult)\
                               .then_inc(filt_done, 1)
                    dve.wait_ge(filt_done, 4)
                    dve.memset(filt[0:1, 0, 1, :], 0.0).then_inc(filt_done, 1)
                    dve.wait_ge(filt_done, 5)
                    dve.tensor_tensor(hsum[:, :, :], filt[:, :, 0, :], filt[:, :, 1, :], ALU.add).then_inc(filt_done, 1)
                    dve.tensor_tensor(hdif[:, :, :], filt[:, :, 0, :], filt[:, :, 1, :], ALU.subtract)\
                       .then_inc(filt_done, 1)
                    dve.wait_ge(filt_done, 7)
                    dve.tensor_tensor(hsum[0:1, 0, :], hsum[0:1, 0, :], hbias[:, :], ALU.add).then_inc(filt_done, 1)

                phase_loop(dve, ph, main_body(ph), after_first=filter_in_time if ph.name == "w_in" else None)
                if ph.name == "w_in":
                    dve.wait_ge(kf_done, 4)
                    dve.wait_ge(tap_done, 6 * KH)
                    for n in range(4):
                        s, m = n // 2, n % 2
                        part = [ga[0], ua[0]] if n % 2 == 0 else [ga[1], ua[1]]
                        if n >= 2:
                            dve.wait_ge(spec_done, 2 * (n - 1))
                        for cs in range(2):
                            dve.wait_ge(u_mm, 2 * n + cs + 1)
                            b = bank[4 + 2 * (n % 2) + cs]
                            for k in range(2):
                                out = spec[:, s, k, m, :] if cs == 0 else part[k][:, :]
                                dve.tensor_tensor(out, b[:, :], kf[:, k if cs == 0 else 1 - k, m, :], ALU.mult)\
                                   .then_inc(prod_done, 1)
                    for g in range(4):
                        dve.wait_ge(ah_done, g + 1)
                        dve.scalar_tensor_tensor(out=al[:, g, :], in0=bank[2 + g % 2][:, :],
                                                 scalar=col(V_PSCALE + g), in1=ah[:, g, :].bitcast(F32),
                                                 op0=ALU.mult, op1=ALU.subtract).then_inc(al_done, 1)
                    for c in range(KH):
                        dve.wait_ge(inv_mm, c + 1)
                        dve.tensor_tensor(x0[:, c, :], bank[4 + c][:, :], x0[:, c, :], ALU.mult).then_inc(gated, 1)
                        dve.wait_ge(ah_done, 4 + c + 1)
                        dve.tensor_tensor(al[:, 4 + c, :], x0[:, c, :], ah[:, 4 + c, :].bitcast(F32), ALU.subtract)\
                           .then_inc(al_done, 1)

        @block.tensor
        def _(pe):
            def three(out, w, k, b, hi, lo, at, start, stop):
                pe.matmul(out, wh[w][:, k, :], hi[:, at, :], start=start, stop=False)
                pe.matmul(out, wh[w][:, k, :], lo[:, at, :], start=False, stop=False)
                return pe.matmul(out, wl[w][:, k, :], hi[:, at, :], start=False, stop=stop)

            def unit(ph, i, j, waits=None, hooks={}):
                w = split_place(ph, j)[0]
                half = ph.name.startswith("down")
                first = not half or j % 2 == 0
                ends = j in ph.groups_at
                hi, lo = ((hh, hl) if half else (ah, al) if ph.name == "w_out" else (oh, ol) if ph.name == "w_o"
                          else (xh, xl))
                b = unit_bank(ph, j)
                pe.wait_ge(low, ph.unit(i, j) + 1 + LOW_CREDIT)
                if first:
                    g = ph.group(i, ph.groups_at[0] if half and j < 2 else ph.groups_at[1] if half else j)
                    at_start = isinstance(i, int) and i == 0 and j < 2
                    look = (1 if at_start else 3) if len(ph.groups_at) == 4 else 0 if ph.name == "qkv" and j == 0 else 1
                    pe.wait_ge(evac, g - look + EVAC_CREDIT)
                for k in range(ph.kt):
                    if k in hooks:
                        hooks[k]()
                    if waits and waits[k]:
                        pe.wait_ge(*waits[k])
                    last = three(bank[b][:, :], w, k, b, hi, lo, k + (KF // 2 if half and j % 2 else 0),
                                 start=first and k == 0, stop=ends and k == ph.kt - 1)
                last.then_inc(unit_done, 1)

            def norm_mean(norm):
                pe.wait_ge(acc_done, chunk_base(norm) + KD)
                for t in range(TT):
                    last = pe.matmul(bank[7][:, t:t + 1], sqacc[:, t * P:(t + 1) * P], cst[:, C_MEAN:C_MEAN + 1],
                                     start=True, stop=True)
                last.then_inc(mean_mm, 1)

            def norm_spread(norm):
                pe.wait_ge(rwide_done, 2 * norm + 2)
                for t in range(TT):
                    last = pe.matmul(bank[7][:, t * P:(t + 1) * P], rwide[:, t, :], ident, start=True, stop=True)
                last.then_inc(rbc_mm, 1)

            pe.wait_ge(const_in, 16)
            pe.wait_ge(vec_in, 16)
            pe.transpose(bank[7][:, 0:V_ALL], vrow[:, :], cst[0:V_ALL, C_ID:C_ID + V_ALL]).then_inc(vec_mm, 1)
            for d in range(KD):
                if d % 4 == 0:
                    pe.wait_ge(x_in[d // 4 * 2], 16)
                    pe.wait_ge(x_in[d // 4 * 2 + 1], 16)
                if d == 7:
                    pe.wait_ge(vec_done, 1)
                for t in range(TT):
                    last = pe.transpose(bank[d][:, t * P:(t + 1) * P], xrow[:, t, d * P:(d + 1) * P], ident)
                last.then_inc(x_mm, 1)

            def filter_layer(n):
                if n == 0:
                    pe.wait_ge(filt_in, 64)
                else:
                    pe.wait_ge(f_sin, n)
                w, z = ((fw1, zT), (fw2, fh), (fw3, fh))[n]
                pe.matmul(bank[6][0:HID, 0:SEQ], w[:, :], z[:, :], start=True, stop=True).then_inc(f_mm, 1)

            def turn_u(i):
                pe.wait_ge(u_done, i + 1)
                if not isinstance(i, int) or i > 0:
                    pe.wait_ge(ut_done, i)
                    pe.wait_ge(filt_done, 4)
                for t in range(TT):
                    last = pe.transpose(bank[7][:, t * P:(t + 1) * P], up[:, t * P:(t + 1) * P], ident)
                last.then_inc(ut_mm, 1)

            def turn_y(d, s):
                pe.wait_ge(evac, by["down3"].group0 + d + 1 + EVAC_CREDIT)
                pe.wait_ge(y_copied, d - 1 + COPY_CREDIT)
                for t in range(TT):
                    last = pe.transpose(bank[2 + s][:, t * P:(t + 1) * P], ga[s][:, t * P:(t + 1) * P], ident)
                last.then_inc(y_mm, 1)

            def attention(p, projects, attends, last_one):
                ph = by["qkv"]

                def scores(s):
                    n = 4 * (p - 1) + 2 * s
                    pe.wait_ge(s_used, 2 * n + SCORE_CREDIT)
                    for t in range(2):
                        at = s * SEQ + t * P
                        for a_ in range(2):
                            last = pe.matmul(bank[4 + a_][:, t * SEQ:(t + 1) * SEQ], qs[a_ * HD:(a_ + 1) * HD, at:at + P],
                                             kn[a_ * HD:(a_ + 1) * HD, s * SEQ:(s + 1) * SEQ], start=True, stop=True)
                    last.then_inc(s_mm, 2)

                def turn(h):
                    n = 4 * (p - 1) + h
                    pe.wait_ge(p_done, 2 * n + 2)
                    pe.wait_ge(t_done, n - 1 + TURN_CREDIT)
                    for k in range(2):
                        for t in range(2):
                            last = pe.transpose(bank[2 if h % 2 else 6][:, k * SEQ + t * P:k * SEQ + (t + 1) * P],
                                                sc[:, h % 2, t, k * P:(k + 1) * P], ident)
                    last.then_inc(t_mm, 1)

                def values(h):
                    s, a_ = h // 2, h % 2
                    n = 4 * (p - 1) + h
                    pe.wait_ge(t_done, n + 1 + TURN_CREDIT)
                    for k in range(2):
                        last = pe.matmul(bank[7][a_ * HD:(a_ + 1) * HD, s * SEQ:(s + 1) * SEQ],
                                         vs[:, 2 * s + k, a_ * HD:(a_ + 1) * HD], pt[:, h % 2, k, :],
                                         start=(k == 0), stop=(k == 1))
                    last.then_inc(pv_mm, 1)

                def squares_mean():
                    pe.wait_ge(sqq_done, p + 1)
                    pe.wait_ge(sqk_done, p + 1)
                    if attends:
                        pe.wait_ge(vs_done, p)
                    for a_, sq in enumerate((sqq, sqk)):
                        for t in range(TT):
                            at = a_ * 2 * TT + 2 * t
                            last = pe.matmul(bank[3][:, at:at + 2], sq[:, t * P:(t + 1) * P], cst[:, C_HEAD:C_HEAD + 2],
                                             start=True, stop=True)
                    last.then_inc(ms_mm, 1)

                def key_factor():
                    pe.wait_ge(kw_done, p + 1)
                    for t in range(TT):
                        last = pe.matmul(bank[3][:, t * P:(t + 1) * P], kwide[:, t, :], ident, start=True, stop=True)
                    last.then_inc(kb_mm, 1)

                def turn_values():
                    pe.wait_ge(evac, ph.group(p, 2) + 1 + EVAC_CREDIT)
                    pe.wait_ge(kn_done, p + 1)
                    for t in range(TT):
                        last = pe.transpose(bank[3][:, t * P:(t + 1) * P], vt[:, t * P:(t + 1) * P], ident)
                    last.then_inc(v_mm, 1)

                def first_scores():
                    pe.wait_ge(kn_done, p)
                    pe.wait_ge(qs_done, p)
                    scores(0)

                def second_scores():
                    turn(0)
                    turn(1)
                    scores(1)

                def first_values():
                    pe.wait_ge(vs_done, p)
                    pe.wait_ge(ol_done, p - 1 + OUT_CREDIT)
                    values(0)
                    values(1)

                if not projects:
                    return {0: first_scores, 3: second_scores, 5: first_values, 6: lambda: (turn(2), turn(3)),
                            7: lambda: (values(2), values(3))}
                if not attends:
                    unit(ph, 0, 0, waits=[(xl_done, chunk_base(4) + k + 1) for k in range(KD)])
                    norm_mean(4)
                    unit(ph, 0, 1, hooks={5: lambda: norm_spread(4)})
                    squares_mean()
                    unit(ph, 0, 2, hooks={6: key_factor})
                    turn_values()
                    return
                unit(ph, p, 0)
                first_scores()
                unit(ph, p, 1)
                second_scores()
                squares_mean()
                first_values()
                unit(ph, p, 2, hooks={6: key_factor})
                turn(2)
                turn(3)
                turn_values()
                values(2)
                values(3)

            for ph in phases:
                name = ph.name
                if name == "qkv":
                    attention(0, True, False, False)
                    with pe.Fori(1, PAIRS) as p:
                        attention(p, True, True, False)
                    continue

                def hooks_at(i, j, name=name):
                    if name == "down0" and isinstance(i, int) and j > 0:
                        return {2: lambda: filter_layer(j - 1)}
                    if name == "down3" and j == 2:
                        return {8: lambda: turn_y(2 * i, 0)}
                    if name == "down3" and j == 0 and not (isinstance(i, int) and i == 0):
                        return {8: lambda: turn_y(2 * i - 1, 1)}
                    return {}

                def first(ph=ph, name=name):
                    if name in NORM_OF:
                        norm = NORM_OF[name]
                        unit(ph, 0, 0, waits=[(xl_done, chunk_base(norm) + k + 1) for k in range(KD)])
                        norm_mean(norm)
                        unit(ph, 0, 1, hooks={5: lambda: norm_spread(norm)})
                        rest = range(2, ph.per)
                    elif name.startswith("down"):
                        done = KF * ffn_of[name]
                        unit(ph, 0, 0, waits=[(hl_done, done + KF - 2)] + [None] * (KF // 2 - 1))
                        unit(ph, 0, 1, waits=[None] * (KF // 2 - 2) + [(hl_done, done + KF - 1), (hl_done, done + KF)],
                             hooks=hooks_at(0, 1))
                        rest = range(2, ph.per)
                    else:
                        of = al_done if name == "w_out" else ol_done
                        extra = 0 if name == "w_out" else OUT_CREDIT
                        unit(ph, 0, 0, waits=[(of, k + 1 + extra) for k in range(KD)],
                             hooks=attention(PAIRS, False, True, False) if name == "w_o" else {})
                        rest = range(1, ph.per)
                    for j in rest:
                        unit(ph, 0, j, hooks=hooks_at(0, j))
                    if name == "w_in":
                        turn_u(0)
                        pe.wait_ge(mix_in, 16 * 7)
                        for n in range(4):
                            t, half = n // 2, n % 2
                            if n == 3:
                                pe.wait_ge(ut_done, 1)
                            pe.matmul(bank[4 + n][:, :], h3[:, t * P:(t + 1) * P], fwo[:, half * HW:(half + 1) * HW],
                                      start=True, stop=True).then_inc(filt_mm, 1)

                def body(i, last, ph=ph, name=name):
                    for j in range(ph.per):
                        unit(ph, i, j, hooks=hooks_at(i, j))
                    if name == "w_in":
                        turn_u(i)

                first()
                with pe.Fori(1, ph.iters) as i:
                    body(i, False)
                if name == "down3":
                    turn_y(KD - 1, 1)
                if name == "w_in":
                    pe.wait_ge(filt_done, 8)
                    for n in range(4):
                        cs, m = n // 2, n % 2
                        if n == 3:
                            pe.wait_ge(ut_done, KH)
                        for t in range(2):
                            last = pe.matmul(bank[4 + n][:, :], dft[:, cs, t, m * P:(m + 1) * P],
                                             (hdif if cs else hsum)[:, t, :], start=(t == 0), stop=(t == 1))
                        last.then_inc(kf_mm, 1)
                    pe.wait_ge(kf_done, 4)
                    for n in range(4):
                        s, m = n // 2, n % 2
                        if n >= 2:
                            pe.wait_ge(prod_done, 4 * (n - 1))
                        for cs in range(2):
                            for t in range(2):
                                last = pe.matmul(bank[4 + 2 * (n % 2) + cs][:, :], dft[:, cs, t, m * P:(m + 1) * P],
                                                 ut[:, 2 * s + t, :], start=(t == 0), stop=(t == 1))
                            last.then_inc(u_mm, 1)
                    pe.wait_ge(evac, ph.group0 + 4 * KH + EVAC_CREDIT)
                    for g in range(4):
                        pe.wait_ge(pooled, g + 1)
                        if g >= 2:
                            pe.wait_ge(al_done, g - 1)
                        pe.matmul(bank[2 + g % 2][:, :].rearrange("p (s t) -> p s t", s=NSEQ), poolw[:, g, :],
                                  ppad[:, g, :, PAD:PAD + SEQ], start=True, stop=True).then_inc(mix_mm, 1)
                    pe.wait_ge(prod_done, 16)
                    for c in range(KH):
                        for s in range(NSEQ):
                            if c == 0:
                                pe.wait_ge(spec_done, 4 * (s + 1))
                            for k in range(4):
                                last = pe.matmul(bank[4 + c][:, s * SEQ:(s + 1) * SEQ],
                                                 spec[:, s, k // 2, k % 2, c * P:(c + 1) * P], idft[:, k, :],
                                                 start=(k == 0), stop=(k == 3))
                        last.then_inc(inv_mm, 1)

        @block.gpsimd
        def _(pool):
            pool.wait_ge(low, LOW_CREDIT)
            for d in range(KD):
                pool.wait_ge(sq_done, d + 1)
                if d:
                    pool.wait_ge(acc_done, d)
                pool.tensor_tensor(sqacc[:, :], sqacc[:, :], sqtmp[:, d % 2, :], ALU.add).then_inc(acc_done, 1)
            ph = by["w_in"]
            pool.wait_ge(unit_done, ph.unit0 + UNIT_CREDIT)
            pool.memset(ppad[:, :, :, :], 0.0).then_inc(pad_done, 1)
            pool.wait_ge(mix_in, 16 * 7)
            step = 0
            for g, w in enumerate(WINDOWS):
                if g:
                    pool.wait_ge(pooled, g)
                pool.wait_ge(evac, ph.group(g, 3) + 1 + EVAC_CREDIT)
                src, lo, hi = ppad[:, g, :, :], 0, PROW
                for n in range(g + 1):
                    back, ahead_ = (1, 0) if n == 0 else (2 ** (n - 1), 2 ** (n - 1))
                    lo, hi = lo + back, hi - ahead_
                    dst = win[n % 2]
                    pool.tensor_tensor(dst[:, :, lo:hi], src[:, :, lo - back:hi - back], src[:, :, lo + ahead_:hi + ahead_],
                                       ALU.add).then_inc(win_step, 1)
                    step += 1
                    pool.wait_ge(win_step, step)
                    src = dst
                mid = src[:, :, PAD:PAD + SEQ]
                inside = ppad[:, g, :, PAD:PAD + SEQ]
                pool.tensor_tensor(mid, mid, icnt[:, g:g + 1, :].to_broadcast([P, NSEQ, SEQ]), ALU.mult)\
                    .then_inc(win_step, 1)
                step += 1
                pool.wait_ge(win_step, step)
                pool.tensor_tensor(inside, mid, inside, ALU.subtract).then_inc(pooled, 1)
            for n in range(4):
                s, m = n // 2, n % 2
                part = [ga[0], ua[0]] if n % 2 == 0 else [ga[1], ua[1]]
                pool.wait_ge(prod_done, 4 * (n + 1))
                pool.tensor_tensor(spec[:, s, 0, m, :], spec[:, s, 0, m, :], part[0][:, :], ALU.subtract)\
                    .then_inc(spec_done, 1)
                pool.tensor_tensor(spec[:, s, 1, m, :], spec[:, s, 1, m, :], part[1][:, :], ALU.add)\
                    .then_inc(spec_done, 1)

            def mask(p, attends):
                pool.wait_ge(braw_in, 32 * (p + 1))
                if attends:
                    pool.wait_ge(mx_done, 4 * p)
                pool.tensor_tensor(bmask[:, :, :].rearrange("p h (r c) -> p (h r) c", c=GRID_W),
                                   braw[:, :, :].rearrange("p h (r c) -> p (h r) c", c=GRID_W),
                                   cst[:, C_MASK:C_MASK + GRID_W].unsqueeze(1).to_broadcast([P, 12, GRID_W]), ALU.add)\
                    .then_inc(mask_done, 1)

            mask(0, False)
            with pool.Fori(1, PAIRS) as p:
                mask(p, True)


def constants():
    small = np.zeros((P, C_ALL), np.float32)
    small[:, C_ID:C_ID + P] = np.eye(P)
    for h in range(2):
        small[h * HD:(h + 1) * HD, C_HEAD + h] = 1.0 / HD
    small[:, C_MEAN] = 1.0 / D
    small[:, C_EPS] = EPS
    t_norm = np.linspace(0.0, 1.0, SEQ, dtype=np.float32)
    small[:, C_T:C_T + 2] = -t_norm.reshape(2, P).T
    q = np.arange(P)[:, None] % GRID_W
    k = np.arange(GRID_W)[None, :]
    start = np.clip(q - NA_COLS // 2, 0, GRID_W - NA_COLS)
    small[:, C_MASK:C_MASK + GRID_W] = np.where((k >= start) & (k < start + NA_COLS), 0.0, -1e30)
    t, m = np.arange(SEQ), np.arange(NFREQ)
    angle = 2.0 * np.pi * (((2 * m[:, None] + 1) * t[None, :]) % (4 * SEQ)) / (4 * SEQ)
    trig = np.stack([np.cos(angle), np.sin(angle)])
    dft = np.zeros((P, 3, 2, 2, SEQ), np.float32)
    dft[:, 0] = trig.transpose(0, 2, 1).reshape(2, 2, P, NFREQ).transpose(2, 0, 1, 3)
    dft[:, 1] = (trig / NFREQ).reshape(2, 2, P, SEQ).transpose(2, 0, 1, 3)
    for g, w in enumerate(WINDOWS):
        lo, hi = np.clip(t - w // 2, 0, SEQ - 1), np.clip(t + w - w // 2 - 1, 0, SEQ - 1)
        dft[:, 2, g // 2, g % 2] = 1.0 / (hi - lo + 1)
    bands = np.linspace(1e-4, 15, 16, dtype=np.float32)
    angles = (np.float32(2.0 * np.pi / SEQ) * np.arange(SEQ, dtype=np.float32)[:, None]) * bands[None, :]
    z = np.concatenate([t_norm[:, None], np.cos(angles), -np.sin(angles)], axis=-1)
    return {"c_small": small, "c_dft": dft, "c_z": np.ascontiguousarray(z.T.astype(np.float32))}


_INS = ["x_prompt", "x_sample", "norm_g", "ffn_w_gate", "ffn_w_up", "ffn_w_down", "w_in_ab", "pool_w", "pool_scale",
        "short_w", "short_b", "filt_w1", "filt_b1", "filt_w2", "filt_b2", "filt_w3", "filt_b3", "filt_freq",
        "filt_w_out", "filt_deltas", "hyena_bias", "w_out_ab", "w_qkv", "q_norm_g", "k_norm_g", "rpb", "w_o"]


def parameter_rows(g):
    rows = [g["norm_g"].reshape(-1, P), g["pool_scale"].reshape(-1, P), g["short_w"].reshape(-1, P),
            g["short_b"].reshape(-1, P)]
    rows += [np.tile(g[name], (1, 2)) for name in ("q_norm_g", "k_norm_g", "filt_b1", "filt_b2", "filt_b3", "filt_freq")]
    return np.concatenate(rows)


def kernel(**inputs):
    import concourse.bacc as bacc
    from concourse.bass_utils import run_bass_kernel_spmd

    nc = bacc.Bacc("TRN2", target_bir_lowering=False, num_devices=1)
    given = {name: np.ascontiguousarray(inputs[name]) for name in _INS}
    given.update(constants(), v_params=parameter_rows(given))
    arrays = {f"in_{name}": v for name, v in given.items()}
    args = {name: nc.dram_tensor(f"in_{name}", v.shape, mybir.dt.from_np(v.dtype), kind="ExternalInput").ap()
            for name, v in given.items()}
    outs = [nc.dram_tensor(name, (1, SEQ, D), F32, kind="ExternalOutput").ap() for name in ("y_prompt", "y_sample")]
    build_trunk(nc, args, *outs)
    got = run_bass_kernel_spmd(nc, [arrays], core_ids=[0]).results[0]
    return got["y_prompt"], got["y_sample"]
```

```python
from contextlib import ExitStack

import numpy as np

import concourse.bass as bass
from concourse import mybir

F32 = mybir.dt.float32
F32R = mybir.dt.float32r
ACT = mybir.ActivationFunctionType
ALU = mybir.AluOpType
AX = mybir.AxisListType

P = 128
D = 1024
KD = D // P
FF = 2816
KF = FF // P
SEQ = 256
NSEQ = 2
TOK = NSEQ * SEQ
TT = TOK // P
EPS = 1e-6
HEADS = 16
HD = 64
PAIRS = HEADS // 2
GRID_W = 64
ROWS = SEQ // GRID_W
RPB_R, RPB_C = 15, 31
DR = 2 * ROWS - 1
NA_COLS = 16
WINDOWS = (2, 4, 8, 16)
HW = 512
KH = HW // P
EMB, HID = 33, 64
NFREQ = SEQ
PAD = 8
PROW = SEQ + 2 * PAD
MAGIC = 1.5 * 2.0 ** 23
TWO_PI = 2.0 * np.pi
PI_A = 6.28125
PI_B = float(np.float32(np.round((TWO_PI - PI_A) * 2.0 ** 21) / 2.0 ** 21))
PI_C = float(np.float32(TWO_PI - PI_A - PI_B))
SIN_MAX = 3.1415925

C_ID, C_HEAD, C_EPS, C_T, C_MASK, C_ALL = 0, 128, 130, 131, 133, 197
V_NORM, V_PSCALE, V_SW, V_SB, V_GQ, V_GK, V_B1, V_FREQ, V_ALL = 0, 48, 52, 88, 100, 101, 102, 105, 106
UNIT_CREDIT, EVAC_CREDIT, LOW_CREDIT = 2, 2, 3
SCORE_CREDIT, TURN_CREDIT, VALUE_CREDIT, OUT_CREDIT, COPY_CREDIT, STORE_CREDIT = 4, 2, 2, 1, 1, 16


class Phase:

    def __init__(self, name, iters, slots, ktiles, groups_at):
        self.name, self.iters, self.slots, self.kt, self.groups_at = name, iters, slots, ktiles, groups_at
        self.per = slots
        self.gper = len(groups_at)

    def unit(self, i, j):
        return self.unit0 + self.per * i + j

    def group(self, i, j):
        return self.group0 + self.gper * i + self.groups_at.index(j)


def plan():
    up = lambda n: Phase(f"up{n}", KF // 2, 4, KD, [0, 1, 2, 3])
    down = lambda n: Phase(f"down{n}", KD // 2, 4, KF // 2, [1, 3])
    phases = [up(0), down(0), Phase("w_in", KH, 4, KD, [0, 1, 2, 3]), Phase("w_out", 2, 4, KD, [0, 1, 2, 3]),
              up(1), down(1), up(2), down(2), Phase("qkv", PAIRS, 3, KD, [0, 1, 2]),
              Phase("w_o", 2, 4, KD, [0, 1, 2, 3]), up(3), down(3)]
    unit, group, uses = 0, KD, [0] * 4
    for n, ph in enumerate(phases):
        ph.unit0, ph.group0, ph.uses0 = unit, group, list(uses)
        unit += ph.iters * ph.per
        group += ph.iters * ph.gper
        for s in range(ph.slots):
            uses[s] += ph.iters
        ph.next = phases[n + 1] if n + 1 < len(phases) else None
    return phases


def build_trunk(nc, a, y_prompt, y_sample):
    phases = plan()
    by = {ph.name: ph for ph in phases}
    NEXT_NORM = {"down0": 1, "w_out": 2, "down1": 3, "down2": 4, "w_o": 5}
    NORM_OF = {"up0": 0, "w_in": 1, "up1": 2, "up2": 3, "qkv": 4, "up3": 5}
    ffn_of = {"up0": 0, "down0": 0, "up1": 1, "down1": 1, "up2": 2, "down2": 2, "up3": 3, "down3": 3}

    wg = a["ffn_w_gate"].rearrange("l j (k p) f -> (l j) p k f", p=P)
    wu = a["ffn_w_up"].rearrange("l j (k p) f -> (l j) p k f", p=P)
    wd = a["ffn_w_down"].rearrange("l j (k p) d -> (l j) p k d", p=P)
    w_in = a["w_in_ab"].rearrange("o (k p) f -> (o p) k f", p=P)
    w_out = a["w_out_ab"].rearrange("o (k p) f -> (o p) k f", p=P)
    w_qkv = a["w_qkv"].rearrange("o (k p) f -> (o p) k f", p=P)
    w_o = a["w_o"].rearrange("o (k p) f -> (o p) k f", p=P)
    bias_dram = nc.dram_tensor("bias_by_column", [GRID_W, HEADS, DR * GRID_W], F32).ap()

    with ExitStack() as ctx:
        def sb(name, shape, dt=F32, where=ctx):
            return where.enter_context(nc.sbuf_tensor(name, shape, dt))

        def sem(name):
            return ctx.enter_context(nc.semaphore(name))

        x = sb("x", [P, KD, TOK])
        xh = sb("xh", [P, KD, TOK], F32R)
        xl = sb("xl", [P, KD, TOK], F32R)
        raw = [sb(f"raw{s}", [P, KF // 2, P]) for s in range(4)]
        wh = [sb(f"wh{s}", [P, KF // 2, P], F32R) for s in range(2)]
        wl = [sb(f"wl{s}", [P, KF // 2, P], F32R) for s in range(2)]
        rbc = sb("rbc", [P, TOK])
        sqacc = sb("sqacc", [P, TOK])
        sqtmp = sb("sqtmp", [P, 2, TOK])
        ga = [sb(f"ga{s}", [P, TOK]) for s in range(2)]
        ua = [sb(f"ua{s}", [P, TOK]) for s in range(2)]
        mean_of = sb("mean_of", [P, P])
        cst = sb("cst", [P, C_ALL])
        vrow = sb("vrow", [V_ALL, P])
        vec = sb("vec", [P, V_ALL])
        gqk = sb("gqk", [P, 1])
        zT, fw1, fw2, fw3 = sb("zT", [EMB, SEQ]), sb("fw1", [EMB, HID]), sb("fw2", [HID, HID]), sb("fw3", [HID, HID])
        h3 = sb("h3", [HID, SEQ])
        fa, fk, fh = ga[0][0:HID, 0:SEQ], ga[1][0:HID, 0:SEQ], ua[0][0:HID, 0:SEQ]
        ident = cst[:, C_ID:C_ID + P]

        def region(rows):
            own = ExitStack()
            got = [sb(*r, where=own) for r in rows]
            own.close()
            return got

        hh, hl = region([("hh", [P, KF, TOK], F32R), ("hl", [P, KF, TOK], F32R)])
        (xrow,) = region([("xrow", [P, TT, D])])
        own = ExitStack()
        dft = sb("dft", [P, 2, 2, NFREQ], where=own)
        idft = sb("idft", [P, 4, SEQ], where=own)
        icnt = sb("icnt", [P, 4, SEQ], where=own)
        kf = sb("kf", [P, 2, 2, HW], where=own)
        x0 = sb("x0", [P, KH, TOK], where=own)
        ppad = sb("ppad", [P, 4, NSEQ, PROW], where=own)
        win = [sb(f"win{s}", [P, NSEQ, PROW], where=own) for s in range(2)]
        up = sb("up", [P, TOK], where=own)
        poolw = sb("poolw", [P, 4, P], where=own)
        inner = ExitStack()
        decay, filt = sb("decay", [P, 2, 2, HW], where=inner), sb("filt", [P, 2, 2, HW], where=inner)
        inner.close()
        spec = sb("spec", [P, NSEQ, 2, 2, HW], where=own)
        inner = ExitStack()
        absd, hsum = sb("absd", [P, 2 * HW], where=inner), sb("hsum", [P, 2, HW], where=inner)
        hdif, ut = sb("hdif", [P, 2, HW], where=inner), sb("ut", [P, TT, HW], where=inner)
        hbias, fwo = sb("hbias", [1, HW], where=inner), sb("fwo", [HID, 2 * HW], where=inner)
        inner.close()
        ah, al = sb("ah", [P, KD, TOK], F32R, where=own), sb("al", [P, KD, TOK], F32R, where=own)
        own.close()
        (wh2, wl2, qt, kt, vt, sqq, sqk, vs, qh, ql, kh, kl, braw, bmask, sc, pt, oh, ol, rsum, nmax, rqk,
         kwide) = region([
            ("wh2", [P, KD, P], F32R), ("wl2", [P, KD, P], F32R), ("qt", [P, TOK]), ("kt", [P, TOK]), ("vt", [P, TOK]),
            ("sqq", [P, TOK]), ("sqk", [P, TOK]), ("vs", [P, TT, P]),
            ("qh", [P, TOK], F32R), ("ql", [P, TOK], F32R), ("kh", [P, TOK], F32R), ("kl", [P, TOK], F32R),
            ("braw", [P, 2, 6 * GRID_W]), ("bmask", [P, 2, 6 * GRID_W]), ("sc", [P, 4, 2, SEQ]), ("pt", [P, 2, 2, SEQ]),
            ("oh", [P, KD, TOK], F32R), ("ol", [P, KD, TOK], F32R), ("rsum", [P, 2, 2]), ("nmax", [P, 2, 2]),
            ("rqk", [P, 2, TT, 2]), ("kwide", [P, TT, P])])
        wh, wl = wh + [wh2], wl + [wl2]

        bank = [ctx.enter_context(nc.psum_tensor(f"bank{b}", [P, TOK], F32)) for b in range(8)]

        raw_in = [sem(f"raw_in{s}") for s in range(4)]
        const_in, vec_in, filt_in = sem("const_in"), sem("vec_in"), sem("filt_in")
        x_in = [sem(f"x_in{s}") for s in range(TT)]
        mix_in, toep_in, braw_in = sem("mix_in"), sem("toep_in"), sem("braw_in")
        high, low, unit_done, evac = sem("high"), sem("low"), sem("unit_done"), sem("evac")
        xh_done, xl_done, sq_done, acc_done = sem("xh_done"), sem("xl_done"), sem("sq_done"), sem("acc_done")
        mean_mm, std_done, rbc_done, mean_of_done = sem("mean_mm"), sem("std_done"), sem("rbc_done"), sem("mean_of_done")
        silu_done, h_done, hh_done, hl_done = sem("silu_done"), sem("h_done"), sem("hh_done"), sem("hl_done")
        vec_mm, vec_done, f_mm, f_step, f_sin = sem("vec_mm"), sem("vec_done"), sem("f_mm"), sem("f_step"), sem("f_sin")
        f_clamp, x_mm, pv_mm = sem("f_clamp"), sem("x_mm"), sem("pv_mm")
        dec_done, filt_mm, filt_done = sem("dec_done"), sem("filt_mm"), sem("filt_done")
        conv_done, tap_done, u_done, ut_mm, ut_done = (sem("conv_done"), sem("tap_done"), sem("u_done"), sem("ut_mm"),
                                                       sem("ut_done"))
        pad_done, win_step, pooled = sem("pad_done"), sem("win_step"), sem("pooled")
        kf_mm, kf_done, u_mm, prod_done, spec_done = (sem("kf_mm"), sem("kf_done"), sem("u_mm"), sem("prod_done"),
                                                      sem("spec_done"))
        mix_mm, inv_mm, gated, ah_done, al_done = (sem("mix_mm"), sem("inv_mm"), sem("gated"), sem("ah_done"),
                                                   sem("al_done"))
        s_mm, s_used, mx_done, exp_done, rs_done, p_done = (sem("s_mm"), sem("s_used"), sem("mx_done"), sem("exp_done"),
                                                            sem("rs_done"), sem("p_done"))
        t_mm, t_done, oh_done, ol_done = sem("t_mm"), sem("t_done"), sem("oh_done"), sem("ol_done")
        sqq_done, sqk_done, ms_mm, ms_std, kw_done = (sem("sqq_done"), sem("sqk_done"), sem("ms_mm"), sem("ms_std"),
                                                      sem("kw_done"))
        rqk_done = sem("rqk_done")
        kb_mm, kn_done, v_mm, vs_done = sem("kb_mm"), sem("kn_done"), sem("v_mm"), sem("vs_done")
        qh_done, ql_done, kh_done, kl_done = sem("qh_done"), sem("ql_done"), sem("kh_done"), sem("kl_done")
        mask_done, gqk_done, y_mm, y_copied = sem("mask_done"), sem("gqk_done"), sem("y_mm"), sem("y_copied")
        y_out = [sem(f"y_out{s}") for s in range(2)]

        block = ctx.enter_context(nc.Block())

        def settle(eng):
            eng.wait_ge(low, LOW_CREDIT)

        def unit_bank(ph, i, j):
            if ph.name == "qkv":
                return (0, 1, 2 if isinstance(i, int) and i == 0 else 0)[j]
            return j // 2 if ph.name.startswith("down") else j

        def unit_source(ph, i, j):
            if ph.name.startswith("up"):
                return (wu if j % 2 else wg)[ffn_of[ph.name], :, :, bass.ds((2 * i + j // 2) * P, P)]
            if ph.name.startswith("down"):
                return wd[ffn_of[ph.name], :, (j % 2) * (KF // 2):(j % 2 + 1) * (KF // 2),
                          bass.ds((2 * i + j // 2) * P, P)]
            if ph.name == "w_in":
                return w_in[:, :, bass.ds((3 - j) * HW + i * P, P)]
            if ph.name == "qkv":
                return w_qkv[:, :, bass.ds(j * D + i * P, P)]
            return (w_out if ph.name == "w_out" else w_o)[:, :, bass.ds((4 * i + j) * P, P)]

        @block.sync
        def _(sp):
            for n in range(4):
                half = slice(n // 2 * (D // 2), (n // 2 + 1) * (D // 2))
                sp.dma_start(xrow[:, n % 2 * 2:n % 2 * 2 + 2, half],
                             (a["x_sample"] if n % 2 else a["x_prompt"])[0].rearrange("(t p) c -> p t c", p=P)[:, :, half])\
                  .then_inc(x_in[n], 16)

            def load(ph, i):
                for j in range(ph.per):
                    sp.wait_ge(low, ph.unit(i, j) - 2 + LOW_CREDIT)
                    sp.dma_start(raw[j][:, 0:ph.kt, :], unit_source(ph, i, j)).then_inc(raw_in[j], 16)

            for ph in phases:
                if ph.name == "w_in":
                    for i in range(ph.iters):
                        load(ph, i)
                else:
                    with sp.Fori(0, ph.iters) as i:
                        load(ph, i)

        def early(ph, i, j):
            return ph.name == "w_o" and isinstance(i, int) and i == 0 and j == 2

        def split_place(ph, i, j):
            return (j if ph.name == "qkv" or early(ph, i, j) else j % 2), j

        def ahead(ph, i, j, last):
            if j + 2 < ph.per:
                return ph, i, j + 2
            if last:
                return (ph.next, 0, j + 2 - ph.per) if ph.next else (None, 0, 0)
            return ph, i + 1, j + 2 - ph.per

        def split_high(act, ph, i, j):
            if ph is None:
                return
            w, r = split_place(ph, i, j)
            act.wait_ge(raw_in[r], 16 * (ph.uses0[r] + 1 + i))
            back = 2 if early(ph, i, j) else 1
            act.wait_ge(unit_done, ph.unit(i, j) - back + UNIT_CREDIT)
            act.activation(wh[w][:, 0:ph.kt, :], raw[r][:, 0:ph.kt, :], ACT.Copy).then_inc(high, 1)

        def split_low(dve, ph, i, j):
            if ph is None:
                return
            w, r = split_place(ph, i, j)
            dve.wait_ge(high, ph.unit(i, j) + 1)
            dve.tensor_tensor(wl[w][:, 0:ph.kt, :], raw[r][:, 0:ph.kt, :], wh[w][:, 0:ph.kt, :].bitcast(F32),
                              ALU.subtract).then_inc(low, 1)

        def chunk_base(norm):
            return KD * norm

        def out_chunk(ph, i, j):
            return 2 * i + j // 2 if ph.name.startswith("down") else 4 * i + j

        def phase_loop(eng, ph, body, after_first=None, first=0):
            if after_first or ph.name in NORM_OF or ph.name == "w_o":
                body(0, False)
                if after_first:
                    after_first()
                first = 1
            if ph.iters - 1 > first:
                with eng.Fori(first, ph.iters - 1) as i:
                    body(i, False)
            body(ph.iters - 1, True)

        @block.scalar
        def _(act):
            col = lambda n: vec[:, bass.ds(n, 1)]

            act.dma_start(cst[:, :], a["c_small"]).then_inc(const_in, 16)
            act.dma_start(vrow[:, :], a["v_params"]).then_inc(vec_in, 16)
            act.dma_start(zT[:, :], a["c_z"]).then_inc(filt_in, 16)
            act.dma_start(fw1[:, :], a["filt_w1"][0]).then_inc(filt_in, 16)
            act.dma_start(fw2[:, :], a["filt_w2"][0]).then_inc(filt_in, 16)
            act.dma_start(fw3[:, :], a["filt_w3"][0]).then_inc(filt_in, 16)

            def residual(ph, i, j, norm):
                d = out_chunk(ph, i, j)
                act.wait_ge(evac, ph.group(i, j) + 1 + EVAC_CREDIT)
                settle(act)
                residual_parts(norm, d, j // 2 % 2 if ph.name.startswith("down") else j % 2)

            def residual_parts(norm, d, parity):
                act.activation(xh[:, bass.ds(d, 1), :], x[:, bass.ds(d, 1), :], ACT.Copy,
                               scale=col(V_NORM + norm * KD + d)).then_inc(xh_done, 1)
                act.activation(sqtmp[:, parity, :], x[:, bass.ds(d, 1), :], ACT.Square).then_inc(sq_done, 1)

            def norm_std(norm):
                act.wait_ge(mean_mm, norm + 1)
                act.activation(rbc[:, :], bank[7][:, :], ACT.Sqrt, bias=cst[:, C_EPS:C_EPS + 1]).then_inc(std_done, 1)

            def evacuate(ph, i, j):
                if ph.name.startswith("up"):
                    f = 2 * i + j // 2
                    g, u = ga[j // 2], ua[j // 2]
                    if j % 2 == 0:
                        act.wait_ge(evac, ph.group(i, j) + 1 + EVAC_CREDIT)
                        act.activation(g[:, :], g[:, :], ACT.Silu).then_inc(silu_done, 1)
                    else:
                        act.wait_ge(h_done, KF * ffn_of[ph.name] + f + 1)
                        settle(act)
                        act.activation(hh[:, bass.ds(f, 1), :], u[:, :], ACT.Copy).then_inc(hh_done, 1)
                elif ph.name in NEXT_NORM:
                    if j in ph.groups_at:
                        residual(ph, i, j, NEXT_NORM[ph.name])
                elif ph.name == "down3":
                    if j in ph.groups_at:
                        s, d = j // 2, out_chunk(ph, i, j)
                        act.wait_ge(y_mm, d + 1)
                        act.wait_ge(y_out[s], 32 * i + STORE_CREDIT)
                        act.activation(ua[s][:, :], bank[2 + s][:, :], ACT.Copy).then_inc(y_copied, 1)
                        act.wait_ge(y_copied, d + 1 + COPY_CREDIT)
                        for n, y in enumerate((y_prompt, y_sample)):
                            act.dma_start(y[0].rearrange("(t p) c -> p t c", p=P)[:, :, bass.ds(d * P, P)],
                                          ua[s][:, n * SEQ:(n + 1) * SEQ].rearrange("p (t c) -> p t c", t=2))\
                               .then_inc(y_out[s], 16)
                elif ph.name == "w_in":
                    if j < 3:
                        at = (2 - j) * KH + i
                        dst = x0[:, bass.ds(i, 1), :] if j == 2 else ua[j][:, :]
                        act.wait_ge(evac, ph.group(i, j) + 1 + EVAC_CREDIT)
                        settle(act)
                        act.activation(dst, ga[j % 2][:, :], ACT.Identity, bias=col(V_SB + at),
                                       scale=col(V_SW + 3 * KH + at)).then_inc(conv_done, 1)
                    else:
                        act.wait_ge(ut_mm, i + 1)
                        settle(act)
                        act.activation(ut[:, :, bass.ds(i * P, P)], bank[7][:, :].rearrange("p (t c) -> p t c", t=TT),
                                       ACT.Copy).then_inc(ut_done, 1)

            for d in range(KD):
                act.wait_ge(evac, d + 1 + EVAC_CREDIT)
                if d >= 2:
                    act.wait_ge(acc_done, d - 1)
                residual_parts(0, d, d % 2)
                if d == 1:
                    split_high(act, phases[0], 0, 0)
                if d == 4:
                    split_high(act, phases[0], 0, 1)
            for r in range(DR):
                src = bass.AP(a["rpb"].tensor, (RPB_R // 2 - ROWS + 1 + r) * RPB_C + RPB_C // 2,
                              [[RPB_R * RPB_C, HEADS], [-1, GRID_W], [1, GRID_W]])
                act.dma_start(bias_dram[:, :, r * GRID_W:(r + 1) * GRID_W].rearrange("q h c -> h q c"), src)\
                   .then_inc(toep_in, 16)

            def attention(p, projects, attends, last):
                ph = by["qkv"]
                if projects:
                    if attends:
                        act.wait_ge(mask_done, p)
                    else:
                        act.wait_ge(toep_in, 16 * DR)
                    for half in range(2):
                        act.dma_start(braw[half * HD:(half + 1) * HD, :, :],
                                      bias_dram[:, bass.ds(2 * p, 2), (1 - half) * GRID_W:(7 - half) * GRID_W])\
                           .then_inc(braw_in, 16)
                    split_high(act, *ahead(ph, p, 0, last))
                    if not attends:
                        norm_std(NORM_OF["qkv"])
                    act.wait_ge(evac, ph.group(p, 0) + 1 + EVAC_CREDIT)
                    act.activation(sqq[:, :], qt[:, :], ACT.Square).then_inc(sqq_done, 1)

                def exps(h):
                    n = 4 * (p - 1) + h
                    act.wait_ge(mx_done, n + 1)
                    for t in range(2):
                        act.activation(sc[:, h, t, :], sc[:, h, t, :], ACT.Exp, bias=nmax[:, h % 2, t:t + 1],
                                       accum_out=rsum[:, h % 2, t:t + 1]).then_inc(exp_done, 1)

                def probs_t(h):
                    n = 4 * (p - 1) + h
                    act.wait_ge(t_mm, n + 1)
                    act.wait_ge(pv_mm, n - 1 + VALUE_CREDIT)
                    turned = bank[2 if h % 2 else 6][:, :].rearrange("p (k q) -> p k q", k=2)
                    act.activation(pt[:, h % 2, :, :], turned, ACT.Copy)\
                       .then_inc(t_done, 1)

                if attends:
                    exps(0)
                    exps(1)
                if projects:
                    split_high(act, *ahead(ph, p, 1, last))
                    act.wait_ge(evac, ph.group(p, 1) + 1 + EVAC_CREDIT)
                    act.activation(sqk[:, :], kt[:, :], ACT.Square).then_inc(sqk_done, 1)
                if attends and projects:
                    probs_t(0)
                    probs_t(1)
                    exps(2)
                    exps(3)
                elif attends:
                    exps(2)
                    exps(3)
                    probs_t(0)
                    probs_t(1)
                    split_high(act, by["w_o"], 0, 2)
                if projects:
                    act.wait_ge(ms_mm, p + 1)
                    act.activation(rqk[:, :, :, :], bank[3][:, 0:4 * TT].rearrange("p (a t h) -> p a t h", a=2, t=TT),
                                   ACT.Sqrt, bias=cst[:, C_EPS:C_EPS + 1]).then_inc(ms_std, 1)
                    if attends:
                        act.wait_ge(s_mm, 4 * p)
                    act.activation(qh[:, :], qt[:, :], ACT.Copy).then_inc(qh_done, 1)
                    act.wait_ge(kn_done, p + 1)
                    act.activation(kh[:, :], kt[:, :], ACT.Copy).then_inc(kh_done, 1)
                    split_high(act, *ahead(ph, p, 2, last))
                if attends:
                    probs_t(2)
                    probs_t(3)
                if projects:
                    act.wait_ge(v_mm, p + 1)
                    if attends:
                        act.wait_ge(pv_mm, 4 * p + VALUE_CREDIT)
                    act.activation(vs[:, :, :], bank[3][:, :].rearrange("p (t c) -> p t c", t=TT), ACT.Copy)\
                       .then_inc(vs_done, 1)
                if attends:
                    act.wait_ge(pv_mm, 4 * p + VALUE_CREDIT)
                    settle(act)
                    act.activation(oh[:, bass.ds(p - 1, 1), :], bank[7][:, :], ACT.Copy).then_inc(oh_done, 1)

            def main_body(ph):
                def body(i, last):
                    for j in range(ph.per):
                        if last and ph.next:
                            evacuate(ph, i, j)
                        if not early(ph, i, j + 2):
                            split_high(act, *ahead(ph, i, j, last))
                        if ph.name in NORM_OF and isinstance(i, int) and i == 0 and j < 2:
                            if j == 0:
                                norm_std(NORM_OF[ph.name])
                            else:
                                evacuate(ph, i, 0)
                                evacuate(ph, i, 1)
                        elif not last or not ph.next:
                            evacuate(ph, i, j)
                return body

            for ph in phases:
                if ph.name == "w_in":
                    act.wait_ge(unit_done, ph.unit0 + UNIT_CREDIT)
                    act.dma_start(absd[:, :], a["filt_deltas"].to_broadcast([P, 2 * HW])).then_inc(mix_in, 16)
                    act.dma_start(fwo[:, :], a["filt_w_out"][0]).then_inc(mix_in, 16)
                    act.dma_start(hbias[:, :], a["hyena_bias"]).then_inc(mix_in, 16)
                    act.dma_start(poolw[:, :, :], a["pool_w"][0].rearrange("g c d -> c g d")).then_inc(mix_in, 16)
                    act.dma_start(dft[:, :, :, :], a["c_dft"][:, 0]).then_inc(mix_in, 16)
                    act.dma_start(idft[:, :, :], a["c_dft"][:, 1].rearrange("p a b m -> p (a b) m")).then_inc(mix_in, 16)
                    act.dma_start(icnt[:, :, :], a["c_dft"][:, 2].rearrange("p a b m -> p (a b) m")).then_inc(mix_in, 16)
                if ph.name == "down0":
                    for j in range(4):
                        split_high(act, *ahead(ph, 0, j, False))
                        evacuate(ph, 0, j)
                        if j < 3:
                            act.wait_ge(f_step, 6 * (j + 1))
                            act.activation((fh if j < 2 else h3)[:, :], fa[:, :], ACT.Sin).then_inc(f_sin, 1)
                    phase_loop(act, ph, main_body(ph), first=1)
                    continue
                if ph.name == "qkv":
                    attention(0, True, False, False)
                    with act.Fori(1, PAIRS - 1) as p:
                        attention(p, True, True, False)
                    attention(PAIRS - 1, True, True, True)
                    attention(PAIRS, False, True, False)
                    continue

                def decays():
                    act.wait_ge(mix_in, 16 * 7)
                    act.activation(absd[:, :], absd[:, :], ACT.Abs).then_inc(dec_done, 1)
                    act.wait_ge(dec_done, 1)
                    for t in range(2):
                        act.activation(decay[:, t, :, :].rearrange("p a c -> p (a c)"), absd[:, :], ACT.Exp,
                                       scale=cst[:, C_T + t:C_T + t + 1]).then_inc(dec_done, 1)

                phase_loop(act, ph, main_body(ph), after_first=decays if ph.name == "w_in" else None)
                if ph.name == "w_in":
                    for n in range(4):
                        act.wait_ge(kf_mm, n + 1)
                        act.activation(kf[:, n // 2, n % 2, :], bank[4 + n][:, :], ACT.Copy).then_inc(kf_done, 1)
                    for g in range(4):
                        act.wait_ge(mix_mm, g + 1)
                        act.activation(ah[:, g, :], bank[g][:, :], ACT.Copy,
                                       scale=col(V_PSCALE + g)).then_inc(ah_done, 1)
                    for c in range(KH):
                        act.wait_ge(gated, c + 1)
                        act.activation(ah[:, 4 + c, :], x0[:, c, :], ACT.Copy).then_inc(ah_done, 1)
            for s in range(2):
                act.wait_ge(y_out[s], 16 * KD + STORE_CREDIT)

        @block.vector
        def _(dve):
            col = lambda n, rows=P: vec[0:rows, bass.ds(n, 1)]

            dve.memset(sqacc[:, :], 0.0).then_inc(low, LOW_CREDIT)
            dve.memset(mean_of[:, :], 1.0 / D).then_inc(mean_of_done, 1)
            for n, (s, credit) in enumerate(((unit_done, UNIT_CREDIT), (evac, EVAC_CREDIT), (s_used, SCORE_CREDIT),
                                             (t_done, TURN_CREDIT), (pv_mm, VALUE_CREDIT), (ol_done, OUT_CREDIT),
                                             (y_copied, COPY_CREDIT), (y_out[0], STORE_CREDIT), (y_out[1], STORE_CREDIT))):
                dve.memset(sqtmp[:, 0, n:n + 1], 0.0).then_inc(s, credit)
            dve.wait_ge(low, LOW_CREDIT)
            dve.wait_ge(vec_mm, 1)
            dve.tensor_copy(vec[:, :], bank[7][:, 0:V_ALL]).then_inc(vec_done, 1)
            dve.wait_ge(vec_done, 1)
            dve.scalar_tensor_tensor(out=gqk[:, :], in0=vec[:, V_GQ:V_GQ + 1], scalar=HD ** -0.5,
                                     in1=vec[:, V_GK:V_GK + 1], op0=ALU.mult, op1=ALU.mult).then_inc(gqk_done, 1)

            def filter_layer(n):
                s = 6 * n
                dve.wait_ge(f_mm, n + 1)
                dve.tensor_scalar(fa[:, :], bank[6][0:HID, 0:SEQ], col(V_B1 + n, HID), col(V_FREQ, HID),
                                  ALU.add, ALU.mult).then_inc(f_step, 1)
                dve.wait_ge(f_step, s + 1)
                dve.tensor_scalar(fk[:, :], fa[:, :], 1.0 / TWO_PI, MAGIC, ALU.mult, ALU.add).then_inc(f_step, 1)
                dve.wait_ge(f_step, s + 2)
                dve.tensor_scalar(fk[:, :], fk[:, :], MAGIC, None, ALU.subtract).then_inc(f_step, 1)
                for m, part in enumerate((PI_A, PI_B, PI_C)):
                    dve.wait_ge(f_step, s + 3 + m)
                    ins = dve.scalar_tensor_tensor(out=fa[:, :], in0=fk[:, :], scalar=-part, in1=fa[:, :],
                                                   op0=ALU.mult, op1=ALU.add)
                    if m < 2:
                        ins.then_inc(f_step, 1)
                    else:
                        ins.then_inc(f_clamp, 1)
                dve.wait_ge(f_clamp, n + 1)
                dve.tensor_scalar(fa[:, :], fa[:, :], SIN_MAX, -SIN_MAX, ALU.min, ALU.max).then_inc(f_step, 1)

            def part_low(norm, d):
                dve.wait_ge(xh_done, chunk_base(norm) + d + 1)
                dve.scalar_tensor_tensor(out=xl[:, bass.ds(d, 1), :], in0=x[:, bass.ds(d, 1), :],
                                         scalar=col(V_NORM + norm * KD + d), in1=xh[:, bass.ds(d, 1), :].bitcast(F32),
                                         op0=ALU.mult, op1=ALU.subtract).then_inc(xl_done, 1)

            def residual_low(norm, d, parity):
                part_low(norm, d)
                dve.wait_ge(sq_done, chunk_base(norm) + d + 1)
                dve.wait_ge(acc_done, chunk_base(norm) + d)
                dve.tensor_tensor(sqacc[:, :], sqacc[:, :], sqtmp[:, parity, :], ALU.add).then_inc(acc_done, 1)

            def norm_factor(norm):
                dve.wait_ge(std_done, norm + 1)
                dve.reciprocal(rbc[:, :], rbc[:, :]).then_inc(rbc_done, 1)
                dve.wait_ge(rbc_done, 2 * norm + 1)

            def sums_cleared(norm):
                dve.memset(sqacc[:, :], 0.0).then_inc(rbc_done, 1)
                dve.wait_ge(rbc_done, 2 * norm + 2)

            def scaled(ph, i, j, out, b, shape=None):
                dve.wait_ge(unit_done, ph.unit(i, j) + 1 + UNIT_CREDIT)
                src, r = bank[b][:, :], rbc[:, :]
                if shape:
                    src, r = src.rearrange(shape, s=NSEQ), r.rearrange(shape, s=NSEQ)
                dve.tensor_tensor(out, src, r, ALU.mult).then_inc(evac, 1)

            def evacuate(ph, i, j):
                if ph.name.startswith("up"):
                    n, f = KF * ffn_of[ph.name], 2 * i + j // 2
                    g, u = ga[j // 2], ua[j // 2]
                    scaled(ph, i, j, (u if j % 2 else g)[:, :], j)
                    if j % 2:
                        dve.wait_ge(silu_done, n + f + 1)
                        dve.wait_ge(evac, ph.group(i, j) + 1 + EVAC_CREDIT)
                        dve.tensor_tensor(u[:, :], g[:, :], u[:, :], ALU.mult).then_inc(h_done, 1)
                        dve.wait_ge(hh_done, n + f + 1)
                        dve.tensor_tensor(hl[:, bass.ds(f, 1), :], u[:, :], hh[:, bass.ds(f, 1), :].bitcast(F32),
                                          ALU.subtract).then_inc(hl_done, 1)
                elif ph.name == "w_in":
                    if j == 3:
                        scaled(ph, i, j, ppad[:, bass.ds(i, 1), :, PAD:PAD + SEQ].rearrange("p o s t -> p (o s) t"), 3,
                               "p (s t) -> p s t")
                        return
                    n = 3 * i + j
                    src = ga[j % 2]
                    if not isinstance(n, int) or n > 0:
                        dve.wait_ge(tap_done, 2 * n)
                    scaled(ph, i, j, src[:, :], j)
                    dst = x0[:, bass.ds(i, 1), :] if j == 2 else ua[j][:, :]
                    dst = dst.rearrange("p o (s t) -> p (o s) t" if j == 2 else "p (s t) -> p s t", s=NSEQ)
                    src = src[:, :].rearrange("p (s t) -> p s t", s=NSEQ)
                    at = (2 - j) * KH + i
                    dve.wait_ge(conv_done, n + 1)
                    dve.scalar_tensor_tensor(out=dst[:, :, 1:SEQ], in0=src[:, :, 0:SEQ - 1], scalar=col(V_SW + at),
                                             in1=dst[:, :, 1:SEQ], op0=ALU.mult, op1=ALU.add).then_inc(tap_done, 1)
                    dve.wait_ge(tap_done, 2 * n + 1)
                    dve.scalar_tensor_tensor(out=dst[:, :, 0:SEQ - 1], in0=src[:, :, 1:SEQ],
                                             scalar=col(V_SW + 6 * KH + at), in1=dst[:, :, 0:SEQ - 1],
                                             op0=ALU.mult, op1=ALU.add).then_inc(tap_done, 1)
                    if j == 1:
                        dve.wait_ge(tap_done, 2 * n + 2)
                        dve.tensor_tensor(up[:, :], ua[0][:, :], ua[1][:, :], ALU.mult).then_inc(u_done, 1)
                elif j in ph.groups_at:
                    d = out_chunk(ph, i, j)
                    parity = j // 2 % 2 if ph.name.startswith("down") else j % 2
                    factor = 0.5 if ph.name.startswith("down") else 1.0
                    b = unit_bank(ph, i, j)
                    dve.wait_ge(unit_done, ph.unit(i, j) + 1 + UNIT_CREDIT)
                    out = ga[parity][:, :] if ph.name == "down3" else x[:, bass.ds(d, 1), :]
                    dve.scalar_tensor_tensor(out=out, in0=bank[b][:, :], scalar=factor, in1=x[:, bass.ds(d, 1), :],
                                             op0=ALU.mult, op1=ALU.add).then_inc(evac, 1)
                    if ph.name != "down3":
                        residual_low(NEXT_NORM[ph.name], d, parity)

            for d in range(KD):
                dve.wait_ge(x_mm, d + 1)
                dve.tensor_copy(x[:, d, :], bank[d][:, :]).then_inc(evac, 1)
            split_low(dve, phases[0], 0, 0)
            for d in range(KD):
                part_low(0, d)
                if d == 4:
                    split_low(dve, phases[0], 0, 1)

            def attention(p, projects, attends, last):
                ph = by["qkv"]

                def maxima(h):
                    s, a_ = h // 2, h % 2
                    n = 4 * (p - 1) + h
                    dve.wait_ge(s_mm, n + 1)
                    for t in range(2):
                        dve.scalar_tensor_tensor(out=sc[:, h, t, :], in0=bank[4 + h % 2][:, t * SEQ:(t + 1) * SEQ],
                                                 scalar=rqk[:, 0, 2 * s + t, a_:a_ + 1],
                                                 in1=bmask[:, a_, (2 - 2 * t) * GRID_W:(6 - 2 * t) * GRID_W],
                                                 op0=ALU.mult, op1=ALU.add).then_inc(s_used, 1)
                    dve.wait_ge(s_used, 2 * (n + 1) + SCORE_CREDIT)
                    dve.tensor_reduce(nmax[:, h % 2, :], sc[:, h, :, :], AX.X, ALU.max, negate=True)\
                       .then_inc(mx_done, 1)

                def normalise(h):
                    n = 4 * (p - 1) + h
                    dve.wait_ge(exp_done, 2 * n + 2)
                    dve.reciprocal(rsum[:, h % 2, :], rsum[:, h % 2, :]).then_inc(rs_done, 1)
                    dve.wait_ge(rs_done, n + 1)
                    for t in range(2):
                        dve.tensor_scalar(sc[:, h, t, :], sc[:, h, t, :], rsum[:, h % 2, t:t + 1], None,
                                          ALU.mult).then_inc(p_done, 1)

                if projects:
                    if attends:
                        dve.wait_ge(ql_done, p)
                        scaled(ph, p, 0, qt[:, :], 0)
                    split_low(dve, *ahead(ph, p, 0, last))
                    if not attends:
                        norm_factor(NORM_OF["qkv"])
                        scaled(ph, p, 0, qt[:, :], 0)
                        sums_cleared(NORM_OF["qkv"])
                if attends:
                    dve.wait_ge(mask_done, p)
                    maxima(0)
                    maxima(1)
                    normalise(0)
                    normalise(1)
                if projects:
                    if attends:
                        dve.wait_ge(kl_done, p)
                    scaled(ph, p, 1, kt[:, :], 1)
                    split_low(dve, *ahead(ph, p, 1, last))
                if attends:
                    maxima(2)
                    maxima(3)
                    normalise(2)
                    normalise(3)
                    if not projects:
                        split_low(dve, by["w_o"], 0, 2)
                if projects:
                    dve.wait_ge(ms_std, p + 1)
                    dve.reciprocal(rqk[:, :, :, :], rqk[:, :, :, :]).then_inc(rqk_done, 1)
                    dve.wait_ge(rqk_done, p + 1)
                    dve.tensor_copy(kwide[:, :, :].rearrange("p t (h c) -> p t h c", h=2),
                                    rqk[:, 1, :, :].unsqueeze(3).to_broadcast([P, TT, 2, HD])).then_inc(kw_done, 1)
                    dve.wait_ge(kb_mm, p + 1)
                    dve.scalar_tensor_tensor(out=kt[:, :], in0=kt[:, :], scalar=gqk[:, 0:1], in1=bank[3][:, :],
                                             op0=ALU.mult, op1=ALU.mult).then_inc(kn_done, 1)
                    if attends:
                        dve.wait_ge(v_mm, p)
                    scaled(ph, p, 2, vt[:, :], unit_bank(ph, p, 2))
                    split_low(dve, *ahead(ph, p, 2, last))
                if attends:
                    dve.wait_ge(oh_done, p)
                    dve.tensor_tensor(ol[:, bass.ds(p - 1, 1), :], bank[7][:, :],
                                      oh[:, bass.ds(p - 1, 1), :].bitcast(F32), ALU.subtract).then_inc(ol_done, 1)

            def main_body(ph):
                def body(i, last):
                    for j in range(ph.per):
                        if last and ph.next:
                            evacuate(ph, i, j)
                        if not early(ph, i, j + 2):
                            split_low(dve, *ahead(ph, i, j, last))
                        if ph.name in NORM_OF and isinstance(i, int) and i == 0 and j < 2:
                            if j == 0:
                                norm_factor(NORM_OF[ph.name])
                            else:
                                evacuate(ph, i, 0)
                                evacuate(ph, i, 1)
                                sums_cleared(NORM_OF[ph.name])
                        elif not last or not ph.next:
                            evacuate(ph, i, j)
                return body

            for ph in phases:
                if ph.name == "w_in":
                    dve.wait_ge(pad_done, 1)
                if ph.name == "down0":
                    for j in range(4):
                        split_low(dve, *ahead(ph, 0, j, False))
                        evacuate(ph, 0, j)
                        if j < 3:
                            filter_layer(j)
                    phase_loop(dve, ph, main_body(ph), first=1)
                    continue
                if ph.name == "qkv":
                    attention(0, True, False, False)
                    with dve.Fori(1, PAIRS - 1) as p:
                        attention(p, True, True, False)
                    attention(PAIRS - 1, True, True, True)
                    attention(PAIRS, False, True, False)
                    continue

                def filter_in_time():
                    for t in range(2):
                        for half in range(2):
                            n = 2 * t + half
                            dve.wait_ge(filt_mm, n + 1)
                            dve.wait_ge(dec_done, 2 + t)
                            dve.scalar_tensor_tensor(out=filt[:, t, half, :], in0=decay[:, t, half, :], scalar=0.05,
                                                     in1=bank[4 + n][:, :], op0=ALU.add, op1=ALU.mult)\
                               .then_inc(filt_done, 1)
                    dve.wait_ge(filt_done, 4)
                    dve.memset(filt[0:1, 0, 1, :], 0.0).then_inc(filt_done, 1)
                    dve.wait_ge(filt_done, 5)
                    dve.tensor_tensor(hsum[:, :, :], filt[:, :, 0, :], filt[:, :, 1, :], ALU.add).then_inc(filt_done, 1)
                    dve.tensor_tensor(hdif[:, :, :], filt[:, :, 0, :], filt[:, :, 1, :], ALU.subtract)\
                       .then_inc(filt_done, 1)
                    dve.wait_ge(filt_done, 7)
                    dve.tensor_tensor(hsum[0:1, 0, :], hsum[0:1, 0, :], hbias[:, :], ALU.add).then_inc(filt_done, 1)

                phase_loop(dve, ph, main_body(ph), after_first=filter_in_time if ph.name == "w_in" else None)
                if ph.name == "w_in":
                    dve.wait_ge(kf_done, 4)
                    dve.wait_ge(tap_done, 6 * KH)
                    for n in range(4):
                        s, m = n // 2, n % 2
                        part = [ga[0], ua[0]] if n % 2 == 0 else [ga[1], ua[1]]
                        if n >= 2:
                            dve.wait_ge(spec_done, 2 * (n - 1))
                        for cs in range(2):
                            dve.wait_ge(u_mm, 2 * n + cs + 1)
                            b = bank[4 + 2 * (n % 2) + cs]
                            for k in range(2):
                                out = spec[:, s, k, m, :] if cs == 0 else part[k][:, :]
                                dve.tensor_tensor(out, b[:, :], kf[:, k if cs == 0 else 1 - k, m, :], ALU.mult)\
                                   .then_inc(prod_done, 1)
                    for g in range(4):
                        dve.wait_ge(ah_done, g + 1)
                        dve.scalar_tensor_tensor(out=al[:, g, :], in0=bank[g][:, :],
                                                 scalar=col(V_PSCALE + g), in1=ah[:, g, :].bitcast(F32),
                                                 op0=ALU.mult, op1=ALU.subtract).then_inc(al_done, 1)
                    for c in range(KH):
                        dve.wait_ge(inv_mm, c + 1)
                        dve.tensor_tensor(x0[:, c, :], bank[4 + c][:, :], x0[:, c, :], ALU.mult).then_inc(gated, 1)
                        dve.wait_ge(ah_done, 4 + c + 1)
                        dve.tensor_tensor(al[:, 4 + c, :], x0[:, c, :], ah[:, 4 + c, :].bitcast(F32), ALU.subtract)\
                           .then_inc(al_done, 1)

        @block.tensor
        def _(pe):
            def three(out, w, k, b, hi, lo, at, start, stop, between=None):
                pe.matmul(out, wh[w][:, k, :], hi[:, at, :], start=start, stop=False)
                if between:
                    pe.wait_ge(*between)
                pe.matmul(out, wh[w][:, k, :], lo[:, at, :], start=False, stop=False)
                return pe.matmul(out, wl[w][:, k, :], hi[:, at, :], start=False, stop=stop)

            def bank_read(ph, i, j):
                at_start = isinstance(i, int) and i == 0 and j < 2
                if ph.name == "w_o" and at_start and j == 0:
                    return evac, ph.group0 + EVAC_CREDIT
                if ph.name == "qkv":
                    look = 1 if j or at_start else 2 if isinstance(i, int) and i == 1 else 0
                    if j == 2 and isinstance(i, int) and i == 0:
                        look = 3
                else:
                    look = 1 if at_start or len(ph.groups_at) == 2 else 3
                return evac, ph.group(i, ph.groups_at[j // 2] if ph.name.startswith("down") else j) - look + EVAC_CREDIT

            def unit(ph, i, j, waits=None, hooks={}, ks=None):
                w = split_place(ph, i, j)[0]
                half = ph.name.startswith("down")
                first = not half or j % 2 == 0
                ends = j in ph.groups_at
                hi, lo = ((hh, hl) if half else (ah, al) if ph.name == "w_out" else (oh, ol) if ph.name == "w_o"
                          else (xh, xl))
                b = unit_bank(ph, i, j)
                ks = ks or range(ph.kt)
                if ks[0] == 0:
                    pe.wait_ge(low, ph.unit(i, j) + 1 + LOW_CREDIT)
                if ks[0] == 0 and first and (ph.name == "qkv" or isinstance(i, int) and i == 0 and j == 0):
                    pe.wait_ge(*bank_read(ph, i, j))
                after = None
                if ph.name != "qkv" and ends:
                    after = bank_read(ph, i + (j + 1) // ph.per, (j + 1) % ph.per)
                for k in ks:
                    if k in hooks:
                        hooks[k]()
                    if waits and waits[k]:
                        pe.wait_ge(*waits[k])
                    last = three(bank[b][:, :], w, k, b, hi, lo, k + (KF // 2 if half and j % 2 else 0),
                                 start=first and k == 0, stop=ends and k == ph.kt - 1,
                                 between=after if k == ph.kt - 1 else None)
                if ks[-1] == ph.kt - 1:
                    last.then_inc(unit_done, 1)

            def norm_mean(norm):
                pe.wait_ge(mean_of_done, 1)
                pe.wait_ge(acc_done, chunk_base(norm) + KD)
                pe.matmul(bank[7][:, :], mean_of[:, :], sqacc[:, :], start=True, stop=True).then_inc(mean_mm, 1)

            pe.wait_ge(const_in, 16)
            pe.wait_ge(vec_in, 16)
            pe.transpose(bank[7][:, 0:V_ALL], vrow[:, :], cst[0:V_ALL, C_ID:C_ID + V_ALL]).then_inc(vec_mm, 1)
            for d in range(KD):
                if d % 4 == 0:
                    pe.wait_ge(x_in[d // 4 * 2], 16)
                    pe.wait_ge(x_in[d // 4 * 2 + 1], 16)
                if d == 7:
                    pe.wait_ge(vec_done, 1)
                for t in range(TT):
                    last = pe.transpose(bank[d][:, t * P:(t + 1) * P], xrow[:, t, d * P:(d + 1) * P], ident)
                last.then_inc(x_mm, 1)

            def filter_layer(n):
                if n == 0:
                    pe.wait_ge(filt_in, 64)
                else:
                    pe.wait_ge(f_sin, n)
                w, z = ((fw1, zT), (fw2, fh), (fw3, fh))[n]
                pe.matmul(bank[6][0:HID, 0:SEQ], w[:, :], z[:, :], start=True, stop=True).then_inc(f_mm, 1)

            def turn_u(i):
                pe.wait_ge(u_done, i + 1)
                if not isinstance(i, int) or i > 0:
                    pe.wait_ge(ut_done, i)
                    pe.wait_ge(filt_done, 4)
                for t in range(TT):
                    last = pe.transpose(bank[7][:, t * P:(t + 1) * P], up[:, t * P:(t + 1) * P], ident)
                last.then_inc(ut_mm, 1)

            def turn_y(d, s):
                pe.wait_ge(evac, by["down3"].group0 + d + 1 + EVAC_CREDIT)
                pe.wait_ge(y_copied, d - 1 + COPY_CREDIT)
                for t in range(TT):
                    last = pe.transpose(bank[2 + s][:, t * P:(t + 1) * P], ga[s][:, t * P:(t + 1) * P], ident)
                last.then_inc(y_mm, 1)

            def attention(p, projects, attends, last_one):
                ph = by["qkv"]

                def scores(s):
                    n = 4 * (p - 1) + 2 * s
                    pe.wait_ge(s_used, 2 * n + SCORE_CREDIT)
                    for t in range(2):
                        at = s * SEQ + t * P
                        for a_ in range(2):
                            rows, out = slice(a_ * HD, (a_ + 1) * HD), bank[4 + a_][:, t * SEQ:(t + 1) * SEQ]
                            keys = slice(s * SEQ, (s + 1) * SEQ)
                            pe.matmul(out, qh[rows, at:at + P], kh[rows, keys], start=True, stop=False)
                            pe.matmul(out, qh[rows, at:at + P], kl[rows, keys], start=False, stop=False)
                            last = pe.matmul(out, ql[rows, at:at + P], kh[rows, keys], start=False, stop=True)
                    last.then_inc(s_mm, 2)

                def turn(h):
                    n = 4 * (p - 1) + h
                    pe.wait_ge(p_done, 2 * n + 2)
                    pe.wait_ge(t_done, n - 1 + TURN_CREDIT)
                    for k in range(2):
                        for t in range(2):
                            last = pe.transpose(bank[2 if h % 2 else 6][:, k * SEQ + t * P:k * SEQ + (t + 1) * P],
                                                sc[:, h, t, k * P:(k + 1) * P], ident)
                    last.then_inc(t_mm, 1)

                def values(pair, h):
                    s, a_ = h // 2, h % 2
                    n = 4 * pair + h
                    pe.wait_ge(t_done, n + 1 + TURN_CREDIT)
                    for k in range(2):
                        last = pe.matmul(bank[7][a_ * HD:(a_ + 1) * HD, s * SEQ:(s + 1) * SEQ],
                                         vs[:, 2 * s + k, a_ * HD:(a_ + 1) * HD], pt[:, h % 2, k, :],
                                         start=(k == 0), stop=(k == 1))
                    last.then_inc(pv_mm, 1)

                def squares_mean():
                    pe.wait_ge(sqq_done, p + 1)
                    pe.wait_ge(sqk_done, p + 1)
                    if attends:
                        pe.wait_ge(vs_done, p)
                    for a_, sq in enumerate((sqq, sqk)):
                        for t in range(TT):
                            at = a_ * 2 * TT + 2 * t
                            last = pe.matmul(bank[3][:, at:at + 2], sq[:, t * P:(t + 1) * P], cst[:, C_HEAD:C_HEAD + 2],
                                             start=True, stop=True)
                    last.then_inc(ms_mm, 1)

                def key_factor(pair=p):
                    pe.wait_ge(kw_done, pair + 1)
                    for t in range(TT):
                        last = pe.matmul(bank[3][:, t * P:(t + 1) * P], kwide[:, t, :], ident, start=True, stop=True)
                    last.then_inc(kb_mm, 1)

                def turn_values():
                    pe.wait_ge(evac, by["qkv"].group(p - 1, 2) + 1 + EVAC_CREDIT)
                    pe.wait_ge(kn_done, p)
                    for t in range(TT):
                        last = pe.transpose(bank[3][:, t * P:(t + 1) * P], vt[:, t * P:(t + 1) * P], ident)
                    last.then_inc(v_mm, 1)

                def first_scores():
                    pe.wait_ge(kl_done, p)
                    pe.wait_ge(ql_done, p)
                    scores(0)

                def second_scores():
                    turn(0)
                    turn(1)
                    scores(1)

                def first_values():
                    pe.wait_ge(vs_done, p)
                    pe.wait_ge(ol_done, p - 1 + OUT_CREDIT)
                    values(p - 1, 0)
                    values(p - 1, 1)

                def second_values(pair):
                    values(pair, 2)
                    values(pair, 3)

                def leftovers():
                    turn_values()
                    if not isinstance(p, int) or p > 1:
                        second_values(p - 2)

                if not projects:
                    ph, ks = by["w_o"], range(KD - 1)
                    parts = [(ol_done, k + 1 + OUT_CREDIT) for k in range(KD)]
                    unit(ph, 0, 0, waits=parts, ks=ks, hooks={1: leftovers, 2: first_scores, 6: lambda: scores(1)})
                    pe.wait_ge(evac, ph.group0 - 1 + EVAC_CREDIT)
                    unit(ph, 0, 1, ks=ks, hooks={0: lambda: (turn(0), turn(1)), 3: first_values,
                                                 4: lambda: (turn(2), turn(3)), 5: lambda: second_values(p - 1)})
                    for j in range(2):
                        unit(ph, 0, j, waits=parts, ks=[KD - 1])
                    return
                if not attends:
                    unit(ph, 0, 0, waits=[(xl_done, chunk_base(4) + k + 1) for k in range(KD)])
                    unit(ph, 0, 1, hooks={1: lambda: norm_mean(4)})
                    unit(ph, 0, 2, hooks={6: squares_mean})
                    return
                if isinstance(p, int):
                    unit(ph, p, 0, hooks={1: lambda: key_factor(0), 4: leftovers})
                else:
                    unit(ph, p, 0, hooks={2: leftovers})
                first_scores()
                unit(ph, p, 1)
                unit(ph, p, 2, hooks={1: second_scores, 4: first_values, 5: squares_mean, 7: key_factor})
                turn(2)
                turn(3)

            for ph in phases:
                name = ph.name
                if name == "qkv":
                    attention(0, True, False, False)
                    attention(1, True, True, False)
                    with pe.Fori(2, PAIRS) as p:
                        attention(p, True, True, False)
                    continue

                def hooks_at(i, j, name=name):
                    if name == "down0" and isinstance(i, int) and j > 0:
                        return {2: lambda: filter_layer(j - 1)}
                    if name == "down3" and j == 2:
                        return {8: lambda: turn_y(2 * i, 0)}
                    if name == "down3" and j == 0 and not (isinstance(i, int) and i == 0):
                        return {8: lambda: turn_y(2 * i - 1, 1)}
                    return {}

                def first(ph=ph, name=name):
                    if name in NORM_OF:
                        norm = NORM_OF[name]
                        unit(ph, 0, 0, waits=[(xl_done, chunk_base(norm) + k + 1) for k in range(KD)])
                        unit(ph, 0, 1, hooks={1: lambda: norm_mean(norm)})
                        rest = range(2, ph.per)
                    elif name.startswith("down"):
                        done = KF * ffn_of[name]
                        unit(ph, 0, 0, waits=[(hl_done, done + KF - 2)] + [None] * (KF // 2 - 1))
                        unit(ph, 0, 1, waits=[None] * (KF // 2 - 2) + [(hl_done, done + KF - 1), (hl_done, done + KF)],
                             hooks=hooks_at(0, 1))
                        rest = range(2, ph.per)
                    else:
                        if name == "w_o":
                            attention(PAIRS, False, True, False)
                            rest = range(2, ph.per)
                        else:
                            unit(ph, 0, 0, waits=[(al_done, k + 1) for k in range(KD)])
                            rest = range(1, ph.per)
                    for j in rest:
                        unit(ph, 0, j, hooks=hooks_at(0, j))
                    if name == "w_in":
                        turn_u(0)
                        pe.wait_ge(mix_in, 16 * 7)
                        for n in range(4):
                            t, half = n // 2, n % 2
                            if n == 3:
                                pe.wait_ge(ut_done, 1)
                            pe.matmul(bank[4 + n][:, :], h3[:, t * P:(t + 1) * P], fwo[:, half * HW:(half + 1) * HW],
                                      start=True, stop=True).then_inc(filt_mm, 1)

                def body(i, last, ph=ph, name=name):
                    for j in range(ph.per):
                        unit(ph, i, j, hooks=hooks_at(i, j))
                    if name == "w_in":
                        turn_u(i)

                first()
                with pe.Fori(1, ph.iters) as i:
                    body(i, False)
                if name == "down3":
                    turn_y(KD - 1, 1)
                if name == "w_in":
                    pe.wait_ge(filt_done, 8)
                    for n in range(4):
                        cs, m = n // 2, n % 2
                        if n == 3:
                            pe.wait_ge(ut_done, KH)
                        for t in range(2):
                            last = pe.matmul(bank[4 + n][:, :], dft[:, cs, t, m * P:(m + 1) * P],
                                             (hdif if cs else hsum)[:, t, :], start=(t == 0), stop=(t == 1))
                        last.then_inc(kf_mm, 1)
                    for n in range(4):
                        s, m = n // 2, n % 2
                        if n < 2:
                            pe.wait_ge(kf_done, 2 * (n + 1))
                        else:
                            pe.wait_ge(prod_done, 4 * (n - 1))
                        for cs in range(2):
                            for t in range(2):
                                last = pe.matmul(bank[4 + 2 * (n % 2) + cs][:, :], dft[:, cs, t, m * P:(m + 1) * P],
                                                 ut[:, 2 * s + t, :], start=(t == 0), stop=(t == 1))
                            last.then_inc(u_mm, 1)
                    pe.wait_ge(evac, ph.group0 + 4 * KH + EVAC_CREDIT)
                    for g in range(4):
                        pe.wait_ge(pooled, g + 1)
                        pe.matmul(bank[g][:, :].rearrange("p (s t) -> p s t", s=NSEQ), poolw[:, g, :],
                                  ppad[:, g, :, PAD:PAD + SEQ], start=True, stop=True).then_inc(mix_mm, 1)
                    pe.wait_ge(prod_done, 16)
                    for c in range(KH):
                        for s in range(NSEQ):
                            if c == 0:
                                pe.wait_ge(spec_done, 4 * (s + 1))
                            for k in range(4):
                                last = pe.matmul(bank[4 + c][:, s * SEQ:(s + 1) * SEQ],
                                                 spec[:, s, k // 2, k % 2, c * P:(c + 1) * P], idft[:, k, :],
                                                 start=(k == 0), stop=(k == 3))
                        last.then_inc(inv_mm, 1)

        @block.gpsimd
        def _(pool):
            pool.wait_ge(low, LOW_CREDIT)
            for d in range(KD):
                pool.wait_ge(sq_done, d + 1)
                if d:
                    pool.wait_ge(acc_done, d)
                pool.tensor_tensor(sqacc[:, :], sqacc[:, :], sqtmp[:, d % 2, :], ALU.add).then_inc(acc_done, 1)
            ph = by["w_in"]
            pool.wait_ge(unit_done, ph.unit0 + UNIT_CREDIT)
            pool.memset(ppad[:, :, :, :], 0.0).then_inc(pad_done, 1)
            pool.wait_ge(mix_in, 16 * 7)
            step = 0
            for g, w in enumerate(WINDOWS):
                if g:
                    pool.wait_ge(pooled, g)
                pool.wait_ge(evac, ph.group(g, 3) + 1 + EVAC_CREDIT)
                src, lo, hi = ppad[:, g, :, :], 0, PROW
                for n in range(g + 1):
                    back, ahead_ = (1, 0) if n == 0 else (2 ** (n - 1), 2 ** (n - 1))
                    lo, hi = lo + back, hi - ahead_
                    dst = win[n % 2]
                    pool.tensor_tensor(dst[:, :, lo:hi], src[:, :, lo - back:hi - back], src[:, :, lo + ahead_:hi + ahead_],
                                       ALU.add).then_inc(win_step, 1)
                    step += 1
                    pool.wait_ge(win_step, step)
                    src = dst
                mid = src[:, :, PAD:PAD + SEQ]
                inside = ppad[:, g, :, PAD:PAD + SEQ]
                pool.tensor_tensor(mid, mid, icnt[:, g:g + 1, :].to_broadcast([P, NSEQ, SEQ]), ALU.mult)\
                    .then_inc(win_step, 1)
                step += 1
                pool.wait_ge(win_step, step)
                pool.tensor_tensor(inside, mid, inside, ALU.subtract).then_inc(pooled, 1)
            for n in range(4):
                s, m = n // 2, n % 2
                part = [ga[0], ua[0]] if n % 2 == 0 else [ga[1], ua[1]]
                pool.wait_ge(prod_done, 4 * (n + 1))
                pool.tensor_tensor(spec[:, s, 0, m, :], spec[:, s, 0, m, :], part[0][:, :], ALU.subtract)\
                    .then_inc(spec_done, 1)
                pool.tensor_tensor(spec[:, s, 1, m, :], spec[:, s, 1, m, :], part[1][:, :], ALU.add)\
                    .then_inc(spec_done, 1)

            def mask(p, attends):
                pool.wait_ge(braw_in, 32 * (p + 1))
                if attends:
                    pool.wait_ge(mx_done, 4 * p)
                pool.tensor_tensor(bmask[:, :, :].rearrange("p h (r c) -> p (h r) c", c=GRID_W),
                                   braw[:, :, :].rearrange("p h (r c) -> p (h r) c", c=GRID_W),
                                   cst[:, C_MASK:C_MASK + GRID_W].unsqueeze(1).to_broadcast([P, 12, GRID_W]), ALU.add)\
                    .then_inc(mask_done, 1)

            def low_parts(p):
                pool.wait_ge(qh_done, p + 1)
                pool.tensor_tensor(ql[:, :], qt[:, :], qh[:, :].bitcast(F32), ALU.subtract).then_inc(ql_done, 1)
                pool.wait_ge(kh_done, p + 1)
                pool.tensor_tensor(kl[:, :], kt[:, :], kh[:, :].bitcast(F32), ALU.subtract).then_inc(kl_done, 1)

            mask(0, False)
            low_parts(0)
            with pool.Fori(1, PAIRS) as p:
                mask(p, True)
                low_parts(p)


def constants():
    small = np.zeros((P, C_ALL), np.float32)
    small[:, C_ID:C_ID + P] = np.eye(P)
    for h in range(2):
        small[h * HD:(h + 1) * HD, C_HEAD + h] = 1.0 / HD
    small[:, C_EPS] = EPS
    t_norm = np.linspace(0.0, 1.0, SEQ, dtype=np.float32)
    small[:, C_T:C_T + 2] = -t_norm.reshape(2, P).T
    q = np.arange(P)[:, None] % GRID_W
    k = np.arange(GRID_W)[None, :]
    start = np.clip(q - NA_COLS // 2, 0, GRID_W - NA_COLS)
    small[:, C_MASK:C_MASK + GRID_W] = np.where((k >= start) & (k < start + NA_COLS), 0.0, -1e30)
    t, m = np.arange(SEQ), np.arange(NFREQ)
    angle = 2.0 * np.pi * (((2 * m[:, None] + 1) * t[None, :]) % (4 * SEQ)) / (4 * SEQ)
    trig = np.stack([np.cos(angle), np.sin(angle)])
    dft = np.zeros((P, 3, 2, 2, SEQ), np.float32)
    dft[:, 0] = trig.transpose(0, 2, 1).reshape(2, 2, P, NFREQ).transpose(2, 0, 1, 3)
    dft[:, 1] = (trig / NFREQ).reshape(2, 2, P, SEQ).transpose(2, 0, 1, 3)
    for g, w in enumerate(WINDOWS):
        lo, hi = np.clip(t - w // 2, 0, SEQ - 1), np.clip(t + w - w // 2 - 1, 0, SEQ - 1)
        dft[:, 2, g // 2, g % 2] = 1.0 / (hi - lo + 1)
    bands = np.linspace(1e-4, 15, 16, dtype=np.float32)
    angles = (np.float32(2.0 * np.pi / SEQ) * np.arange(SEQ, dtype=np.float32)[:, None]) * bands[None, :]
    z = np.concatenate([t_norm[:, None], np.cos(angles), -np.sin(angles)], axis=-1)
    return {"c_small": small, "c_dft": dft, "c_z": np.ascontiguousarray(z.T.astype(np.float32))}


_INS = ["x_prompt", "x_sample", "norm_g", "ffn_w_gate", "ffn_w_up", "ffn_w_down", "w_in_ab", "pool_w", "pool_scale",
        "short_w", "short_b", "filt_w1", "filt_b1", "filt_w2", "filt_b2", "filt_w3", "filt_b3", "filt_freq",
        "filt_w_out", "filt_deltas", "hyena_bias", "w_out_ab", "w_qkv", "q_norm_g", "k_norm_g", "rpb", "w_o"]


def parameter_rows(g):
    rows = [g["norm_g"].reshape(-1, P), g["pool_scale"].reshape(-1, P), g["short_w"].reshape(-1, P),
            g["short_b"].reshape(-1, P)]
    rows += [np.tile(g[name], (1, 2)) for name in ("q_norm_g", "k_norm_g", "filt_b1", "filt_b2", "filt_b3", "filt_freq")]
    return np.concatenate(rows)


def kernel(**inputs):
    import concourse.bacc as bacc
    from concourse.bass_utils import run_bass_kernel_spmd

    nc = bacc.Bacc("TRN2", target_bir_lowering=False, num_devices=1)
    given = {name: np.ascontiguousarray(inputs[name]) for name in _INS}
    given.update(constants(), v_params=parameter_rows(given))
    arrays = {f"in_{name}": v for name, v in given.items()}
    args = {name: nc.dram_tensor(f"in_{name}", v.shape, mybir.dt.from_np(v.dtype), kind="ExternalInput").ap()
            for name, v in given.items()}
    outs = [nc.dram_tensor(name, (1, SEQ, D), F32, kind="ExternalOutput").ap() for name in ("y_prompt", "y_sample")]
    build_trunk(nc, args, *outs)
    got = run_bass_kernel_spmd(nc, [arrays], core_ids=[0]).results[0]
    return got["y_prompt"], got["y_sample"]
```
